# Optimizing a Trainium2 kernel written in Bass

```python
import math
import jax, jax.numpy as jnp
from jax import lax
import numpy as np

D_MODEL = 1024
BATCH = 1
SEQ = 512
DEPTH = 1

ATTN_WIDTH = D_MODEL // 2
ATTN_HEAD_DIM = 64
ATTN_QK_DIM = ATTN_HEAD_DIM // 2
ATTN_HEADS = ATTN_WIDTH // ATTN_HEAD_DIM
POOL_WIDTH = D_MODEL // 4
POOL_WINDOWS = (2, 4, 8, 16)
POOL_GROUPS = len(POOL_WINDOWS)
POOL_GROUP_DIM = POOL_WIDTH // POOL_GROUPS
CONV_WIDTH = D_MODEL // 4
CONV_GROUPS = 4
CONV_K = 3
MIX_WIDTH = ATTN_WIDTH + POOL_WIDTH + CONV_WIDTH
IN_WIDTH = 3 * ATTN_WIDTH + POOL_WIDTH + 3 * CONV_WIDTH
D_FF = ((8 * D_MODEL // 3 + 255) // 256) * 256
Q_BLOCK = 128
EPS = 1e-6


def rmsnorm(x, g):
    xf = x.astype(jnp.float32)
    y = xf * lax.rsqrt(jnp.mean(xf * xf, axis=-1, keepdims=True) + EPS)
    return (y * g.astype(jnp.float32)).astype(x.dtype)

def alibi_slopes(n_heads):
    return jnp.asarray(np.array([2.0 ** (-8.0 * (h + 1) / n_heads) for h in range(n_heads)], dtype=np.float32))

def diff_attention(q, k, v, lam, slopes):
    b_, s_ = q.shape[0], q.shape[1]
    nblk = s_ // Q_BLOCK
    scale = ATTN_QK_DIM ** -0.5
    qb = q.reshape(b_, nblk, Q_BLOCK, ATTN_HEADS, 2, ATTN_QK_DIM).transpose(1, 0, 2, 3, 4, 5)
    kpos = jnp.arange(s_)

    def one_block(args):
        qi, blk = args
        qpos = blk * Q_BLOCK + jnp.arange(Q_BLOCK)
        dist = jnp.abs(qpos[:, None] - kpos[None, :]).astype(jnp.float32)
        bias = -slopes[:, None, None] * dist[None]
        s = jnp.einsum('bqhpd,bkhpd->bphqk', qi, k).astype(jnp.float32) * scale + bias
        p = jax.nn.softmax(s, axis=-1)
        w = p[:, 0] - lam * p[:, 1]
        return jnp.einsum('bhqk,bkhd->bqhd', w.astype(v.dtype), v)

    out = lax.map(one_block, (qb, jnp.arange(nblk)))
    return out.transpose(1, 0, 2, 3, 4).reshape(b_, s_, ATTN_HEADS, ATTN_HEAD_DIM)

def multiscale_pool(u, w_pool, pool_scale):
    b_, s_, _ = u.shape
    uf = u.astype(jnp.float32)
    csum = jnp.concatenate([jnp.zeros((b_, 1, POOL_WIDTH), jnp.float32), jnp.cumsum(uf, axis=1)], axis=1)
    t = jnp.arange(s_)
    pooled = []
    for g, w in enumerate(POOL_WINDOWS):
        cg = csum[..., g * POOL_GROUP_DIM:(g + 1) * POOL_GROUP_DIM]
        lo = jnp.clip(t - w // 2, 0, s_)
        hi = jnp.clip(t + w - w // 2, 0, s_)
        total = jnp.take(cg, hi, axis=1) - jnp.take(cg, lo, axis=1)
        cnt = (hi - lo).astype(jnp.float32)
        pooled.append(total / cnt[None, :, None])
    pooled = jnp.stack(pooled, axis=2)
    diff = pooled - uf.reshape(b_, s_, POOL_GROUPS, POOL_GROUP_DIM)
    mixed = jnp.einsum('bsgc,gcd->bsgd', diff, w_pool.astype(jnp.float32))
    return (mixed.reshape(b_, s_, POOL_WIDTH) * pool_scale.astype(jnp.float32)).astype(u.dtype)

def short_gated_conv(b_gate, c_gate, xh, conv_w):
    u = c_gate * xh
    up = jnp.pad(u, ((0, 0), (1, 1), (0, 0)))
    y = conv_w[0] * up[:, :-2] + conv_w[1] * up[:, 1:-1] + conv_w[2] * up[:, 2:]
    return b_gate * y

def modulate(h, shift, scale):
    return h * (1.0 + scale[:, None, :]) + shift[:, None, :]

def first_inputs(seed: int = 0) -> dict:
    key = jax.random.key(seed)
    ks = jax.random.split(key, 20)
    f32 = jnp.float32
    n = lambda k, shape, s: jax.random.normal(k, shape, f32) * s
    return {
        "x": n(ks[0], (BATCH, SEQ, D_MODEL), 1.0),
        "c": n(ks[1], (BATCH, D_MODEL), 1.0),
        "w_ada": n(ks[2], (DEPTH, D_MODEL, 6 * D_MODEL), D_MODEL ** -0.5),
        "b_ada": n(ks[3], (DEPTH, 6 * D_MODEL), 0.02),
        "g_mix": 1.0 + n(ks[4], (DEPTH, D_MODEL), 0.1),
        "w_in": n(ks[5], (DEPTH, D_MODEL, IN_WIDTH), D_MODEL ** -0.5),
        "lambda_q1": n(ks[6], (DEPTH, ATTN_QK_DIM), 0.1),
        "lambda_k1": n(ks[7], (DEPTH, ATTN_QK_DIM), 0.1),
        "lambda_q2": n(ks[8], (DEPTH, ATTN_QK_DIM), 0.1),
        "lambda_k2": n(ks[9], (DEPTH, ATTN_QK_DIM), 0.1),
        "g_subln": 1.0 + n(ks[10], (DEPTH, ATTN_WIDTH), 0.1),
        "w_pool": n(ks[11], (DEPTH, POOL_GROUPS, POOL_GROUP_DIM, POOL_GROUP_DIM), POOL_GROUP_DIM ** -0.5),
        "pool_scale": 1.0 + n(ks[12], (DEPTH, POOL_WIDTH), 0.1),
        "conv_w": n(ks[13], (DEPTH, CONV_K, CONV_WIDTH), 0.5),
        "w_out": n(ks[14], (DEPTH, MIX_WIDTH, D_MODEL), MIX_WIDTH ** -0.5),
        "g_ffn": 1.0 + n(ks[15], (DEPTH, D_MODEL), 0.1),
        "w_gate_up": n(ks[16], (DEPTH, D_MODEL, 2 * D_FF), D_MODEL ** -0.5),
        "w_down": n(ks[17], (DEPTH, D_FF, D_MODEL), D_FF ** -0.5),
        "g_final": 1.0 + n(ks[18], (D_MODEL,), 0.1),
    }

def first_block(x, c, w_ada, b_ada, g_mix, w_in, lambda_q1, lambda_k1, lambda_q2, lambda_k2,
              g_subln, w_pool, pool_scale, conv_w, w_out, g_ffn, w_gate_up, w_down, g_final):
    b_, s_, _ = x.shape
    slopes = alibi_slopes(ATTN_HEADS)
    c_act = jax.nn.silu(c)
    o_q, o_k, o_v = ATTN_WIDTH, 2 * ATTN_WIDTH, 3 * ATTN_WIDTH
    o_p = o_v + POOL_WIDTH
    o_b, o_c = o_p + CONV_WIDTH, o_p + 2 * CONV_WIDTH
    for l in range(DEPTH):
        mod = c_act @ w_ada[l] + b_ada[l]
        sh1, sc1, gt1, sh2, sc2, gt2 = jnp.split(mod, 6, axis=-1)

        h = modulate(rmsnorm(x, g_mix[l]), sh1, sc1)
        proj = h @ w_in[l]
        q = proj[..., :o_q].reshape(b_, s_, ATTN_HEADS, 2, ATTN_QK_DIM)
        k = proj[..., o_q:o_k].reshape(b_, s_, ATTN_HEADS, 2, ATTN_QK_DIM)
        v = proj[..., o_k:o_v].reshape(b_, s_, ATTN_HEADS, ATTN_HEAD_DIM)
        u_pool = proj[..., o_v:o_p]
        b_gate, c_gate, x_conv = proj[..., o_p:o_b], proj[..., o_b:o_c], proj[..., o_c:]

        lambda_init = 0.8 - 0.6 * math.exp(-0.3 * l)
        lam = (jnp.exp(jnp.sum(lambda_q1[l].astype(jnp.float32) * lambda_k1[l].astype(jnp.float32)))
               - jnp.exp(jnp.sum(lambda_q2[l].astype(jnp.float32) * lambda_k2[l].astype(jnp.float32)))
               + lambda_init)
        attn = diff_attention(q, k, v, lam, slopes)
        attn = rmsnorm(attn, g_subln[l].reshape(ATTN_HEADS, ATTN_HEAD_DIM)) * (1.0 - lambda_init)
        y_a = attn.reshape(b_, s_, ATTN_WIDTH)
        y_b = multiscale_pool(u_pool, w_pool[l], pool_scale[l])
        y_c = short_gated_conv(b_gate, c_gate, x_conv, conv_w[l])

        mixed = jnp.concatenate([y_a, y_b, y_c], axis=-1) @ w_out[l]
        x = x + gt1[:, None, :] * mixed

        h = modulate(rmsnorm(x, g_ffn[l]), sh2, sc2)
        gate, up = jnp.split(h @ w_gate_up[l], 2, axis=-1)
        x = x + gt2[:, None, :] * ((jax.nn.silu(gate) * up) @ w_down[l])

    return rmsnorm(x, g_final)


HEAD_DIM = 64
NA_HEADS = 8
NB_HEADS = 8
NB_KV_HEADS = 2
GRID_W = 64
NA_KH_MAX = 8
NA_KW = 16
WIN = 128
BLOCK = 128
ROPE_THETA = 10000.0
D_FF_2 = 2816

WIDTH_A = NA_HEADS * HEAD_DIM
WIDTH_BQ = NB_HEADS * HEAD_DIM
WIDTH_BKV = NB_KV_HEADS * HEAD_DIM
D_IN = 3 * WIDTH_A + WIDTH_BQ + 2 * WIDTH_BKV + 2 * D_MODEL
SPLITS = (WIDTH_A, 2 * WIDTH_A, 3 * WIDTH_A,
          3 * WIDTH_A + WIDTH_BQ,
          3 * WIDTH_A + WIDTH_BQ + WIDTH_BKV,
          3 * WIDTH_A + WIDTH_BQ + 2 * WIDTH_BKV,
          3 * WIDTH_A + WIDTH_BQ + 2 * WIDTH_BKV + D_MODEL)


def rms_norm(x, g):
    xf = x.astype(jnp.float32)
    y = xf * lax.rsqrt(jnp.mean(xf * xf, axis=-1, keepdims=True) + EPS)
    return (y * g.astype(jnp.float32)).astype(x.dtype)

def swiglu(x, w_gate, w_up, w_down):
    return (jax.nn.silu(x @ w_gate) * (x @ w_up)) @ w_down

def rope(x, pos):
    half = x.shape[-1] // 2
    inv = ROPE_THETA ** (-jnp.arange(half, dtype=jnp.float32) / half)
    ang = pos.astype(jnp.float32)[:, None] * inv[None, :]
    cos = jnp.cos(ang)[None, :, None, :]
    sin = jnp.sin(ang)[None, :, None, :]
    x1 = x[..., :half].astype(jnp.float32)
    x2 = x[..., half:].astype(jnp.float32)
    out = jnp.concatenate([x1 * cos - x2 * sin, x2 * cos + x1 * sin], axis=-1)
    return out.astype(x.dtype)

def neighbourhood_attention_2d(q, k, v, rpb):
    B, T, H, dh = q.shape
    rows = T // GRID_W
    kh = min(NA_KH_MAX, rows)
    q = q.reshape(B, rows, GRID_W, H, dh)
    k = k.reshape(B, rows, GRID_W, H, dh)
    v = v.reshape(B, rows, GRID_W, H, dh)
    cols = jnp.arange(GRID_W)
    col_start = jnp.clip(cols - NA_KW // 2, 0, GRID_W - NA_KW)
    col_idx = col_start[:, None] + jnp.arange(NA_KW)[None, :]
    col_off = col_idx - cols[:, None] + (NA_KW - 1)
    rpb = rpb.astype(jnp.float32)
    scale = dh ** -0.5

    def row_block(args):
        r, q_r = args
        rs = jnp.clip(r - kh // 2, 0, rows - kh)
        k_slab = lax.dynamic_slice_in_dim(k, rs, kh, axis=1)
        v_slab = lax.dynamic_slice_in_dim(v, rs, kh, axis=1)
        k_g = k_slab[:, :, col_idx]
        v_g = v_slab[:, :, col_idx]
        row_off = rs + jnp.arange(kh) - r + (NA_KH_MAX - 1)
        bias = rpb[:, row_off[None, :, None], col_off[:, None, :]]
        s = jnp.einsum('bchd,bicjhd->bhcij', q_r, k_g).astype(jnp.float32) * scale
        s = s + bias[None]
        p = jax.nn.softmax(s.reshape(B, H, GRID_W, kh * NA_KW), axis=-1)
        p = p.reshape(B, H, GRID_W, kh, NA_KW).astype(v.dtype)
        return jnp.einsum('bhcij,bicjhd->bchd', p, v_g)

    out = lax.map(row_block, (jnp.arange(rows), jnp.moveaxis(q, 1, 0)))
    return jnp.moveaxis(out, 0, 1).reshape(B, T, H * dh)

def windowed_gqa_sink(q, k, v, sink):
    B, T, Hq, dh = q.shape
    Hkv = k.shape[2]
    G = Hq // Hkv
    nb = T // BLOCK
    qb = q.reshape(B, nb, BLOCK, Hkv, G, dh)

    def band(a):
        ap = jnp.pad(a, ((0, 0), (BLOCK, BLOCK), (0, 0), (0, 0)))
        ab = ap.reshape(B, nb + 2, BLOCK, Hkv, dh)
        return jnp.concatenate([ab[:, :-2], ab[:, 1:-1], ab[:, 2:]], axis=2)

    kb = band(k)
    vb = band(v)
    qpos = jnp.arange(nb)[:, None] * BLOCK + jnp.arange(BLOCK)[None, :]
    kpos = jnp.arange(nb)[:, None] * BLOCK - BLOCK + jnp.arange(3 * BLOCK)[None, :]
    kp = kpos[:, None, :]
    mask = (jnp.abs(qpos[:, :, None] - kp) <= WIN) & (kp >= 0) & (kp < T)
    s = jnp.einsum('bnqhgd,bnkhd->bnhgqk', qb, kb).astype(jnp.float32) * (dh ** -0.5)
    s = jnp.where(mask[None, :, None, None], s, -jnp.inf)
    sink_l = sink.astype(jnp.float32).reshape(Hkv, G)[None, None, :, :, None, None]
    m = jnp.maximum(jnp.max(s, axis=-1, keepdims=True), sink_l)
    e = jnp.exp(s - m)
    p = e / (jnp.sum(e, axis=-1, keepdims=True) + jnp.exp(sink_l - m))
    o = jnp.einsum('bnhgqk,bnkhd->bnqhgd', p.astype(v.dtype), vb)
    return o.reshape(B, T, Hq * dh)

def second_inputs(seed: int = 0) -> dict:
    key = jax.random.key(seed)
    ks = jax.random.split(key, 20)
    f32 = jnp.float32

    def w(k, shape, fan_in):
        return jax.random.normal(k, shape, f32) * (fan_in ** -0.5)

    def gain(k, shape):
        return 1.0 + 0.02 * jax.random.normal(k, shape, f32)

    return {
        "x": jax.random.normal(ks[0], (BATCH, SEQ, D_MODEL), f32),
        "ffn1_norm": gain(ks[1], (DEPTH, D_MODEL)),
        "ffn1_w_gate": w(ks[2], (DEPTH, D_MODEL, D_FF_2), D_MODEL),
        "ffn1_w_up": w(ks[3], (DEPTH, D_MODEL, D_FF_2), D_MODEL),
        "ffn1_w_down": w(ks[4], (DEPTH, D_FF_2, D_MODEL), D_FF_2),
        "mix_norm": gain(ks[5], (DEPTH, D_MODEL)),
        "w_in": w(ks[6], (DEPTH, D_MODEL, D_IN), D_MODEL),
        "na_rpb": 0.1 * jax.random.normal(ks[7], (DEPTH, NA_HEADS, 2 * NA_KH_MAX - 1, 2 * NA_KW - 1), f32),
        "sink_logit": 0.5 * jax.random.normal(ks[8], (DEPTH, NB_HEADS), f32),
        "w_branch_a": w(ks[9], (DEPTH, WIDTH_A, D_MODEL), WIDTH_A),
        "w_branch_b": w(ks[10], (DEPTH, WIDTH_BQ, D_MODEL), WIDTH_BQ),
        "w_out": w(ks[11], (DEPTH, D_MODEL, D_MODEL), D_MODEL),
        "ffn2_norm": gain(ks[12], (DEPTH, D_MODEL)),
        "ffn2_w_gate": w(ks[13], (DEPTH, D_MODEL, D_FF_2), D_MODEL),
        "ffn2_w_up": w(ks[14], (DEPTH, D_MODEL, D_FF_2), D_MODEL),
        "ffn2_w_down": w(ks[15], (DEPTH, D_FF_2, D_MODEL), D_FF_2),
        "final_norm": gain(ks[16], (D_MODEL,)),
    }

def second_block(x, ffn1_norm, ffn1_w_gate, ffn1_w_up, ffn1_w_down, mix_norm, w_in, na_rpb,
              sink_logit, w_branch_a, w_branch_b, w_out, ffn2_norm, ffn2_w_gate, ffn2_w_up,
              ffn2_w_down, final_norm):
    B, T, _ = x.shape
    pos = jnp.arange(T)
    h = x
    for l in range(DEPTH):
        h = h + 0.5 * swiglu(rms_norm(h, ffn1_norm[l]), ffn1_w_gate[l], ffn1_w_up[l], ffn1_w_down[l])
        u = rms_norm(h, mix_norm[l])
        z = u @ w_in[l]
        qa, ka, va, qb, kb, vb, ga, gb = jnp.split(z, SPLITS, axis=-1)
        qa = qa.reshape(B, T, NA_HEADS, HEAD_DIM)
        ka = ka.reshape(B, T, NA_HEADS, HEAD_DIM)
        va = va.reshape(B, T, NA_HEADS, HEAD_DIM)
        ya = neighbourhood_attention_2d(qa, ka, va, na_rpb[l])
        qb = rope(qb.reshape(B, T, NB_HEADS, HEAD_DIM), pos)
        kb = rope(kb.reshape(B, T, NB_KV_HEADS, HEAD_DIM), pos)
        vb = vb.reshape(B, T, NB_KV_HEADS, HEAD_DIM)
        yb = windowed_gqa_sink(qb, kb, vb, sink_logit[l])
        merged = jax.nn.sigmoid(ga) * (ya @ w_branch_a[l]) + jax.nn.sigmoid(gb) * (yb @ w_branch_b[l])
        h = h + merged @ w_out[l]
        h = h + 0.5 * swiglu(rms_norm(h, ffn2_norm[l]), ffn2_w_gate[l], ffn2_w_up[l], ffn2_w_down[l])
    return rms_norm(h, final_norm)


def setup_inputs(seed=0):
    out = dict(first_inputs(seed))
    for name, value in second_inputs(seed + 1).items():
        if name != "x":
            out[name + "_2"] = value
    return out


def reference(
    x, c, w_ada, b_ada, g_mix, w_in, lambda_q1, lambda_k1, lambda_q2, lambda_k2, g_subln,
    w_pool, pool_scale, conv_w, w_out, g_ffn, w_gate_up, w_down, g_final, ffn1_norm_2,
    ffn1_w_gate_2, ffn1_w_up_2, ffn1_w_down_2, mix_norm_2, w_in_2, na_rpb_2, sink_logit_2,
    w_branch_a_2, w_branch_b_2, w_out_2, ffn2_norm_2, ffn2_w_gate_2, ffn2_w_up_2, ffn2_w_down_2,
    final_norm_2,
):
    x = first_block(
        x, c, w_ada, b_ada, g_mix, w_in, lambda_q1, lambda_k1, lambda_q2, lambda_k2, g_subln,
        w_pool, pool_scale, conv_w, w_out, g_ffn, w_gate_up, w_down, g_final,
    )
    return second_block(
        x, ffn1_norm_2, ffn1_w_gate_2, ffn1_w_up_2, ffn1_w_down_2, mix_norm_2, w_in_2, na_rpb_2,
        sink_logit_2, w_branch_a_2, w_branch_b_2, w_out_2, ffn2_norm_2, ffn2_w_gate_2,
        ffn2_w_up_2, ffn2_w_down_2, final_norm_2,
    )


_drawn_inputs = setup_inputs


def setup_inputs(seed=0):
    import zlib

    import numpy as np

    out = dict(_drawn_inputs(seed))
    spreads = {}
    factors = {'lambda_q1': 8.0,
     'lambda_k1': 8.0,
     'lambda_q2': 5.505,
     'lambda_k2': 8.0,
     'ffn1_norm_2': 6.576,
     'mix_norm_2': 8.0,
     'na_rpb_2': 8.0,
     'sink_logit_2': 8.0,
     'ffn2_norm_2': 19.583,
     'final_norm_2': 7.539}
    for name, (base, spread) in spreads.items():
        noise = np.random.default_rng([zlib.crc32(name.encode()), seed]).standard_normal(out[name].shape)
        drawn = base * np.exp(spread * noise) if base else spread * noise
        out[name] = __import__('jax').numpy.asarray(drawn.astype(out[name].dtype))
    for name, factor in factors.items():
        out[name] = (out[name] * factor).astype(out[name].dtype)
    return out
```

```python
from contextlib import ExitStack, contextmanager

import concourse.bass as bass
import numpy as np
from concourse import mybir

P = 128
T = 512
D = 1024
KD = D // P
TT = T // P
FF = 2816
KF = FF // P
HALF = KF // 2
H = 8
DQ1 = 32
DH = 64
GRID = 64
NEAR_ROWS, NEAR_COLS = 8, 16
DR = 2 * NEAR_ROWS - 1
DC = 2 * NEAR_COLS - 1
WIN = 128
EPS = 1e-6
FAR = 1e30
PAD = GRID - NEAR_COLS
LAMBDA_INIT = 0.2

F32 = mybir.dt.float32
F32R = mybir.dt.float32r
ALU = mybir.AluOpType
ACT = mybir.ActivationFunctionType
BYTES = 4

VECTORS = [("b_ada", 48), ("c", 8), ("g_mix", 8), ("g_subln", 4), ("pool_scale", 2), ("conv_w", 6),
           ("g_ffn", 8), ("g_final", 8), ("ffn1_norm_2", 8), ("mix_norm_2", 8), ("ffn2_norm_2", 8),
           ("final_norm_2", 8)]
ROW_OF, _at = {}, 0
for _name, _rows in VECTORS:
    ROW_OF[_name] = _at
    _at += _rows
N_ROWS = _at

SH1, SC1, GT1, SH2, SC2, GT2 = (KD * j for j in range(6))
N_MOD = 6 * KD


def constants():
    p = np.arange(P)
    out = {"k_ident": np.eye(P, dtype=np.float32)}
    f = p % DH
    turn = np.zeros((P, P), np.float32)
    turn[p, np.where(f < DH // 2, p + DH // 2, p - DH // 2)] = 1.0
    out["k_turn"] = turn
    out["k_dist"] = np.abs(p[:, None] - np.arange(2 * T - P)[None, :] + T - P).astype(np.float32)
    out["k_band"] = np.where(np.abs(p[:, None] + P - np.arange(3 * P)[None, :]) > WIN, FAR, 0.0).astype(np.float32)
    col = p % GRID
    start = np.clip(col - NEAR_COLS // 2, 0, GRID - NEAR_COLS)
    key = np.arange(GRID)[None, :]
    inside = (key >= start[:, None]) & (key < start[:, None] + NEAR_COLS)
    out["k_near"] = np.where(inside, 0.0, FAR).astype(np.float32)
    half = DH // 2
    inv = np.float32(10000.0) ** (-np.arange(half, dtype=np.float32) / np.float32(half))
    ang = np.arange(T, dtype=np.float32)[None, :] * inv[(f % half)][:, None]
    out["k_cos"] = np.cos(ang).astype(np.float32)
    out["k_sin"] = (np.sin(ang) * np.where(f < half, -1.0, 1.0)[:, None]).astype(np.float32)
    t = np.arange(T)
    rows = []
    for w in (2, 4, 8, 16):
        n = np.clip(t + w - w // 2, 0, T) - np.clip(t - w // 2, 0, T)
        rows.append(np.repeat((1.0 / n)[None], DH, 0))
    out["k_count"] = np.stack([np.concatenate(rows[0:2]), np.concatenate(rows[2:4])], 1).astype(np.float32)
    return out


class Count:

    def __init__(self):
        self.n, self.i, self.slope = 0, None, 0

    def now(self, ahead=0):
        v = self.n + ahead
        return v if self.i is None else self.i * self.slope + v


@contextmanager
def repeat(eng, times, slopes):
    before = [(c, c.n, s) for c, s in slopes]
    with eng.Fori(0, times) as i:
        for c, _, s in before:
            c.i, c.slope = i, s
        yield i
    for c, n, s in before:
        assert c.n - n == s, (c.n - n, s)
        c.n, c.i = n + s * times, None


def program(nc, ins, out):
    ctx = ExitStack()
    with ctx:
        def sem(name):
            return ctx.enter_context(nc.semaphore(name))

        BASE = 16512
        END = nc.sbuf_usable_end
        area = {"at": BASE}

        def place(name, shape, dt=F32, at=None):
            size = int(np.prod(shape[1:])) * BYTES
            size += -size % 32
            where = area["at"] if at is None else at
            if at is None:
                area["at"] += size
                assert area["at"] <= END, (name, area["at"], END)
            return nc.alloc_sbuf_tensor_at(name, list(shape), dt, offset=where)

        def region(start, limit, items):
            at, got = start, []
            for name, shape, dt in items:
                size = int(np.prod(shape[1:])) * BYTES
                got.append(place(name, shape, dt, at))
                at += size + (-size % 32)
                assert at <= limit, (name, at, limit)
            return got, at

        x = place("x_res", [P, KD, T])
        o_scaled = place("o_scaled", [P, KD, T], at=area["at"])
        h_hi = place("h_hi", [P, KD, T], F32R)
        h_lo = place("h_lo", [P, KD, T], F32R)
        w_raw = place("w_raw", [P, 2, HALF * P])
        w_hi = place("w_hi", [P, 2, HALF * P], F32R)
        w_lo = place("w_lo", [P, 2, HALF * P], F32R)
        ident = place("ident", [P, P])
        turn_m = place("turn_m", [P, P])
        rows = place("rows", [P, P])
        vcol = place("vcol", [P, P])
        modc = place("modc", [P, N_MOD])
        scale1 = place("scale1", [P, KD])
        scale2 = place("scale2", [P, KD])
        gff = place("gff", [P, KD])
        cact = place("cact", [P, KD])
        small = place("small", [P, 32])
        rcol = place("rcol", [P, 16])
        lamrow = place("lamrow", [P, 200])
        stat = place("stat", [P, 3, 8])
        rsub = place("rsub", [P, 32])
        ms2 = place("ms2", [P, 4])
        sub8 = place("sub8", [P, 4])
        acc = place("acc", [P, 2, T])
        sq = place("sq", [P, 2, 2, T])
        rs = place("rs", [P, T])
        rs_half = place("rs_half", [P, T])
        rs_fin = place("rs_fin", [P, T])
        OVER = area["at"]
        BIG_SIZE = 2 * KF * T * BYTES
        BIG = END - BIG_SIZE
        BIG -= BIG % 32
        BIG_END = BIG + BIG_SIZE

        eps = small[:, 0:1]
        mean_d = small[:, 1:2]
        one = small[0:1, 2:3]
        neg_lam = small[:, 3:4]
        sink = small[:, 4:12]
        neg_sink = small[:, 14:22]
        mean_h = small[:, 12:14]

        (hid_hi, hid_lo), _ = region(BIG, BIG_END, [("hid_hi", [P, KF, T], F32R), ("hid_lo", [P, KF, T], F32R)])
        (t_gate, t_silu, t_hid), _ = region(OVER, BIG, [(n, [P, T], F32) for n in ("t_gate", "t_silu", "t_hid")])
        (x_tok, xn_tok, xn_t, mod_row), at0 = region(BIG, BIG_END, [
            ("x_tok", [P, TT, D], F32), ("xn_tok", [P, TT, D], F32), ("xn_t", [P, KD, T], F32),
            ("mod_row", [1, N_MOD * P], F32)])
        (junk, hm), _ = region(OVER, BIG, [("junk", [P, D], F32), ("hm", [P, 2, T], F32)])
        (q1, k1, v1_hi, v1_lo, wt_hi, wt_lo, o1, p1, alibi, dist), at1 = region(BIG, BIG_END, [
            ("q1", [P, 4, T], F32), ("k1", [P, 4, T], F32), ("v1_hi", [P, TT, T], F32R),
            ("v1_lo", [P, TT, T], F32R), ("wt_hi", [P, 2, TT, 2 * P], F32R),
            ("wt_lo", [P, 2, TT, 2 * P], F32R), ("o1", [P, 4, T], F32), ("p1", [P, 3, 2, T], F32),
            ("alibi", [P, 2, 2 * T - P], F32), ("dist", [P, 2 * T - P], F32)])
        y_side = place("y_side", [P, 4, T], F32, at1)
        assert at1 + 4 * T * BYTES <= BIG_END
        (pool_u, pool_s, pool_d, conv_c, conv_u, wpool_bd), _ = region(OVER, BIG, [
            ("pool_u", [P, T + 16], F32), ("pool_s", [P, 2, T + 16], F32), ("pool_d", [P, T], F32),
            ("conv_c", [P, 2, T], F32), ("conv_u", [P, 2, T + 2], F32), ("wpool_bd", [P, 2, P], F32)])
        pool_t = rs
        count_sb = rs_half[:, :], rs_fin[:, :]
        z_t, z_c = sq[:, 0, 0, :], sq[:, 0, 1, :]
        (cos_sb, sin_sb, band, near_mask, yb_lo, kb), BIG2 = region(OVER, BIG, [
            ("cos_sb", [P, T], F32), ("sin_sb", [P, T], F32),
            ("band", [P, 3 * P], F32), ("near_mask", [P, GRID], F32), ("yb_lo", [P, 4, T], F32R),
            ("kb", [P, T], F32)])
        (qa, ka, va_hi, va_lo, qb, vb_hi, vb_lo, near, wt2_hi, wt2_lo, za, p2), _ = region(BIG2, END, [
            ("qa", [P, 4, T], F32), ("ka", [P, 4, T], F32), ("va_hi", [P, TT, T], F32R),
            ("va_lo", [P, TT, T], F32R), ("qb", [P, 4, T], F32), ("vb_hi", [P, TT, P], F32R),
            ("vb_lo", [P, TT, P], F32R), ("near", [P, 2, DR - 1, GRID], F32),
            ("wt2_hi", [P, 2, TT, 2 * P], F32R), ("wt2_lo", [P, 2, TT, 2 * P], F32R),
            ("za", [P, KD, T], F32), ("p2", [P, 3, T], F32)])
        size4 = 4 * T * BYTES
        ya_hi = place("ya_hi", [P, 4, T], F32R, BIG2)
        ya_lo = place("ya_lo", [P, 4, T], F32R, BIG2 + size4)
        m_hi = place("m_hi", [P, KD, T], F32R, BIG2 + 2 * size4)
        yb_hi = place("yb_hi", [P, 4, T], F32R, BIG2 + 4 * size4)
        WT_AT = BIG2 + 5 * size4 + 2 * TT * P * BYTES + 2 * (DR - 1) * GRID * BYTES
        m_lo = place("m_lo", [P, KD, T], F32R, WT_AT)
        (t_sa, t_sb, t_m), _ = region(WT_AT + 2 * size4 + KD * T * BYTES, END, [
            (n, [P, T], F32) for n in ("t_sa", "t_sb", "t_m")])
        o_tok = place("o_tok", [P, TT, D], at=BIG)
        psum = ctx.enter_context(nc.psum_tensor("psum", [P, 8, T], F32))
        n_rpb = ins["rpb"].shape[0]
        rpb_rows = nc.dram_tensor("rpb_rows", (GRID, n_rpb), F32, kind="Internal").ap()

        S_V, S_Q0, S_MIX1 = 0, 4, 6
        S_OUT1 = 20
        S_GU = [28, 88, 198]
        S_DN = [72, 132, 242]
        S_PROJ2, S_QB, S_MIX2 = 148, 154, 158
        S_MERGE, S_OUT2 = 174, 190
        N_SLABS = 258
        N_ADA = N_MOD
        UN1, UN2 = 32, 64
        N_MIX1 = S_OUT1 - S_MIX1

        def tiles_of(s):
            return HALF if any(a <= s < a + 2 * KD for a in S_DN) else KD

        def pieces_of(s):
            if S_QB <= s < S_QB + 4:
                return 2
            return 3 if S_MERGE <= s < S_OUT2 and s % 2 else 1

        landed_at, total = [], [N_ADA // 2 * 16] * 2
        for s_ in range(N_SLABS):
            total[s_ % 2] += 16 * pieces_of(s_)
            landed_at.append(total[s_ % 2])

        rows_landed, x_landed, const_landed = sem("rows_landed"), sem("x_landed"), sem("const_landed")
        lam_landed, dist_landed, table_landed = sem("lam_landed"), sem("dist_landed"), sem("table_landed")
        rpb_copied = sem("rpb_copied")
        wpool_landed, count_landed, out_landed = sem("wpool_landed"), sem("count_landed"), sem("out_landed")
        raw_landed = [sem("raw_landed0"), sem("raw_landed1")]
        near_landed = [sem("near_landed0"), sem("near_landed1")]
        ada_used, w_high, w_ready, w_used = sem("ada_used"), sem("w_high"), sem("w_ready"), sem("w_used")
        filled = [sem(f"bank_filled{b}") for b in range(8)]
        emptied = [sem(f"bank_emptied{b}") for b in range(8)]
        consts_set, lam_set = sem("consts_set"), sem("lam_set")
        lam_exp, lam_prod = sem("lam_exp"), sem("lam_prod")
        cact_set, x_rms, xn_set, mod_set, x_root = sem("cact_set"), sem("x_rms"), sem("xn_set"), sem("mod_set"), sem("x_root")
        h_high, h_ready = sem("h_high"), sem("h_ready")
        v_high = sem("v_high")
        alibi_set, expd, combined, wt_high = sem("alibi_set"), sem("expd"), sem("combined"), sem("wt_high")
        pads_set, pooled, conv_ready, conved, wpool_set = sem("pads_set"), sem("pooled"), sem("conv_ready"), sem("conved"), sem("wpool_set")
        side_set, o_squared, sub_scaled, y_set = sem("side_set"), sem("o_squared"), sem("sub_scaled"), sem("y_set")
        squared, summed, acc_clear = sem("squared"), sem("summed"), sem("acc_clear")
        cols_set, scale_set, root2 = sem("cols_set"), sem("scale_set"), sem("root2")
        scaled_x = sem("scaled_x")
        gate_scaled, gate_act, hid_set, hid_high, hid_ready = (sem(n) for n in (
            "gate_scaled", "gate_act", "hid_set", "hid_high", "hid_ready"))
        x_new = sem("x_new")
        roped, y2_high = sem("roped"), sem("y2_high")
        expd2, combined2, wt2_high, near_set = sem("expd2"), sem("combined2"), sem("wt2_high"), sem("near_set")
        sa_set, sb_set, merged, m_high, m_ready = sem("sa_set"), sem("sb_set"), sem("merged"), sem("m_high"), sem("m_ready")
        o_final, tok_set = sem("o_final"), [sem("tok_set0"), sem("tok_set1")]
        scored2, branch_set, t_set = sem("scored2"), sem("branch_set"), sem("t_set")
        dve_step, act_step, pool_step = sem("dve_step"), sem("act_step"), sem("pool_step")

        SQUARES = {"out1": 0, "down0": 8, "down1": 24, "out2": 32, "down2": 40}
        NEW_X = {"out1": 0, "down0": 8, "down1": 16, "out2": 24, "down2": 32}
        SUM0 = 2
        GEN = {"proj1": 0, "y": 1, "ffn0": 2, "ffn1": 3, "mix2": 4, "ffn2": 5}

        bank, before, full, free_at = {}, {}, {}, {}
        last_turn, n_full, n_free = {}, [0] * 8, [0] * 8

        def plan(name, b, complete=None, read=None):
            if complete is None:
                n_full[b] += 1
                complete = (filled[b], n_full[b])
            if read is None:
                n_free[b] += 1
                read = (emptied[b], n_free[b])
            bank[name], before[name], full[name], free_at[name] = b, last_turn.get(b), complete, read
            last_turn[b] = name

        def plan_slab(name, b, s, read=None):
            plan(name, b, (w_used, s + 1), read)

        plan("vectors", 7)
        for k in range(KD):
            plan(("x", k), k % 4)
        for k in range(KD):
            plan(("xn", k), 4 + k % 3)
        for r in range(N_ADA // 4):
            plan(("ada", r), r % 2, (ada_used, 4 * r + 4))
        plan("mod", 7)
        for i in range(TT):
            plan_slab(("v1", i), i, S_V + 3)
        plan_slab(("slab", S_Q0), 7, S_Q0)
        plan_slab(("slab", S_Q0 + 1), 6, S_Q0 + 1)
        for u in range(UN1):
            for m in range(2):
                plan(("s1", u, m), 2 * (u % 2) + m)
            plan(("t1", u), 4 + u % 2)
        for g in range(UN1 // 2):
            plan(("o1", g), 6)
        for s_ in range(S_MIX1, S_OUT1):
            plan_slab(("slab", s_), 7, s_)
        plan(("pool", 0), 0)
        plan(("pool", 1), 1)
        plan("sub_sum", 7)
        for c in range(4):
            plan(("sub", c), c, read=(y_set, c + 1))

        def plan_scale(name, nth, two=False):
            plan(("sum", name), 6)
            if two:
                plan(("scale", name), 7)
                plan(("scale2", name), 6, read=(scale_set, nth))
            else:
                plan(("scale", name), 7, read=(scale_set, nth))

        def plan_ffn(f):
            for n in range(KF):
                m, s = KF * f + n + 1, S_GU[f] + 2 * n
                plan_slab(("gate", f, n), 4 if n == 0 else 0, s, (gate_scaled, m - KF) if f else (gate_act, m))
                plan_slab(("up", f, n), 5 if n == 0 else 1, s + 1, (hid_set, m))
            for n in range(KD):
                plan_slab(("down", f, n), 2 + n % 2, S_DN[f] + 2 * n + 1,
                          (t_set, KD * (f - 1) + n + 1) if f else (x_new, NEW_X["down0"] + n + 1))

        for n in range(KD):
            plan_slab(("out1", n), 4 + n % 2, S_OUT1 + n, (x_new, NEW_X["out1"] + n + 1))
        plan_scale("ffn0", 1)
        plan_ffn(0)
        plan_scale("ffn1", 2, two=True)
        plan_ffn(1)
        for i in range(TT):
            plan_slab(("va", i), i, S_PROJ2 + 3)
        plan_scale("mix2", 3)
        plan_slab("vb", 4, S_PROJ2 + 4)
        plan_slab("kb", 5, S_PROJ2 + 5, (roped, 1))
        plan("kb_turn", 6)
        for c in range(4):
            plan_slab(("qb", c), 7 if c % 2 == 0 else 5, S_QB + c, (roped, 3 + 2 * c))
            plan(("qb_turn", c), 4 if c % 2 == 0 else 6)
        for u in range(UN2):
            plan(("s2", u), u % 4, read=None if u < UN2 // 2 else (scored2, u + 1))
            plan(("t2", u), 4 + u % 2)
        for g in range(UN2 // 2):
            plan(("o2", g), 6)
        for s_ in range(S_MIX2, S_MERGE):
            plan_slab(("slab", s_), 7, s_)
        for n in range(KD):
            plan_slab(("gb", n), 0, S_MERGE + 2 * n, (sb_set, n + 1))
            plan(("a", n), 1, read=(branch_set, 2 * n + 1))
            plan_slab(("b", n), 2, S_MERGE + 2 * n + 1, (branch_set, 2 * n + 2))
        for n in range(KD):
            plan_slab(("out2", n), 4 + n % 2, S_OUT2 + n, (x_new, NEW_X["out2"] + n + 1))
        plan_scale("ffn2", 4)
        plan_ffn(2)
        plan(("sum", "last"), 6)
        for i in range(TT):
            for half in range(2):
                plan(("fin", i, half), 2 * i + half)

        def along(value, n, i=None, step=1):
            v = value(n)
            return v if i is None else i * (value(n + step) - v) + v

        def slot_of(n, i=None, step=1):
            return bass.ds(n if i is None else i * step + n, 1)

        N_CONSTS = 7
        YS = [6, 7, 4, 5, 0, 1, 2, 3]
        KINDS1 = [("q", 1), ("k", 1), ("u", 0), ("u", 1), ("q", 2), ("k", 2), ("cg", 0), ("cg", 1),
                  ("q", 3), ("k", 3), ("xc", 0), ("xc", 1), ("bg", 0), ("bg", 1)]

        def unit2(u):
            windowed, v = u < UN2 // 2, u % (UN2 // 2)
            c, j, i = v // 8, v % 8 // 4, v % 4
            if windowed:
                return True, c, j, i, c + 4 * j, list(range(max(0, i - 1), min(TT, i + 2)))
            return False, c, j, i, 2 * c + j, list(range(TT))

        def exps2(u):
            return 2 * (u + 1) if u < UN2 // 2 else UN2 + u + 1 - UN2 // 2

        def wait_filled(eng, name, n=None, i=None, step=1):
            key = name if n is None else (*name, n)
            s_, v = full[key]
            if i is not None:
                v = along(lambda m: full[(*name, m)][1], n, i, step)
            eng.wait_ge(s_, v)
            return bank[key]

        def wait_emptied(eng, name):
            eng.wait_ge(*free_at[name])

        block = ctx.enter_context(nc.Block())

        @block.tensor
        def _(pe):
            def bank_of(name):
                return bank[name]

            def take(name, n=None, i=None, step=1):
                key = name if n is None else (*name, n)
                if i is not None:
                    key = (*name, n)
                    assert before[key] == (*name, n - step)
                    pe.wait_ge(free_at[key][0], along(lambda m: free_at[(*name, m)][1], n - step, i, step))
                elif before[key] is not None:
                    pe.wait_ge(*free_at[before[key]])
                return bank[key]

            def three(o, a_hi, a_lo, b_hi, b_lo, start, stop):
                pe.matmul(o, a_hi, b_hi, start=start, stop=False)
                pe.matmul(o, a_hi, b_lo, start=False, stop=False)
                return pe.matmul(o, a_lo, b_hi, start=False, stop=stop)

            def tile(s, j):
                return w_hi[:, s % 2, P * j:P * j + P], w_lo[:, s % 2, P * j:P * j + P]

            def await_slab(s, i=None, step=1):
                pe.wait_ge(w_ready, s + 1 if i is None else i * step + s + 1)

            def chunk(o, s, js, xs, ready=None, start=True, stop=True):
                last = None
                for n, (j, (b_hi, b_lo)) in enumerate(zip(js, xs)):
                    if ready is not None:
                        pe.wait_ge(ready[0], ready[1] + n + 1)
                    w = tile(s, j)
                    last = three(o, *w, b_hi, b_lo, start and n == 0, stop and n == len(js) - 1)
                return last

            hs = [(h_hi[:, k, :], h_lo[:, k, :]) for k in range(KD)]

            pe.wait_ge(const_landed, 32)
            pe.wait_ge(rows_landed, 16 * len(VECTORS))
            pe.transpose(psum[:, 7, 0:N_ROWS], rows[0:N_ROWS, :], ident[0:N_ROWS, 0:N_ROWS]).then_inc(filled[7], 1)
            pe.wait_ge(x_landed, 16 * TT)
            for src, name in ((x_tok, "x"), (xn_tok, "xn")):
                for k in range(KD):
                    if name == "xn" and k == 0:
                        pe.wait_ge(xn_set, TT)
                    b = take((name, k))
                    for i in range(TT):
                        last = pe.transpose(psum[:, b, P * i:P * i + P], src[:, i, P * k:P * k + P], ident[:, :])
                    last.then_inc(filled[b], 1)

            pe.wait_ge(cact_set, 1)
            def ada_rows(i=None):
                for r in range(2):
                    b = take(("ada",), r, None) if i is None else take(("ada",), r + 2, i, 2)
                    for q in range(4):
                        sl = (4 * r + q) % 2
                        landed = 16 * ((4 * r + q) // 2 + 1)
                        pe.wait_ge(raw_landed[sl], landed if i is None else i * 64 + 64 + landed)
                        for k in range(KD):
                            last = pe.matmul(psum[0:1, b, P * q:P * q + P], cact[:, k:k + 1],
                                             w_raw[:, sl, P * k:P * k + P], start=k == 0, stop=k == KD - 1)
                        last.then_inc(ada_used, 1)

            ada_rows()
            with repeat(pe, N_ADA // 8 - 1, []) as i:
                ada_rows(i)
            wait_emptied(pe, ("ada", N_ADA // 4 - 2))
            wait_emptied(pe, ("ada", N_ADA // 4 - 1))
            b = take("mod")
            pe.wait_ge(consts_set, N_CONSTS)
            for n in range(N_MOD):
                last = pe.matmul(psum[:, b, n:n + 1], mod_row[0:1, P * n:P * n + P], one, start=True, stop=True)
            last.then_inc(filled[b], 1)

            for s in range(S_V, S_V + 4):
                await_slab(s)
                for i in range(TT):
                    b = take(("v1", i)) if s == S_V else i
                    for j in range(2):
                        k = 2 * (s - S_V) + j
                        pe.wait_ge(h_ready, k + 1)
                        ts = slice(P * i, P * i + P)
                        ws = slice(T * j, T * j + T)
                        last = three(psum[:, b, :], h_hi[:, k, ts], h_lo[:, k, ts], w_hi[:, s % 2, ws],
                                     w_lo[:, s % 2, ws], k == 0, k == KD - 1)
                last.then_inc(w_used, 1)

            def whole(name, s, xs=hs, ready=None):
                await_slab(s)
                b = take(name)
                last = chunk(psum[:, b, :], s, range(KD), xs, ready)
                last.then_inc(w_used, 1)

            whole(("slab", S_Q0), S_Q0)
            whole(("slab", S_Q0 + 1), S_Q0 + 1)

            def part(s, q, parts):
                n = KD // parts
                if q == 0:
                    await_slab(s)
                    take(("slab", s))
                b = bank_of(("slab", s))
                last = chunk(psum[:, b, :], s, range(n * q, n * q + n), hs[n * q:n * q + n], None, q == 0, q == parts - 1)
                if q == parts - 1:
                    last.then_inc(w_used, 1)

            for t in range(UN1 + 4):
                if t < UN1:
                    h, i = t // 4, t % 4
                    c = h // 2
                    if t % 8 == 0:
                        wait_emptied(pe, ("slab", S_Q0 if c == 0 else S_MIX1 + 4 * (c - 1)))
                        wait_emptied(pe, ("slab", S_Q0 + 1 if c == 0 else S_MIX1 + 4 * (c - 1) + 1))
                    for m in range(2):
                        b = take(("s1", t, m))
                        r = DH * (h % 2) + DQ1 * m
                        pe.matmul(psum[:, b, :], q1[r:r + DQ1, c, P * i:P * i + P], k1[r:r + DQ1, c, :],
                                  start=True, stop=True).then_inc(filled[b], 1)
                if t < 2 * N_MIX1:
                    part(S_MIX1 + t // 2, t % 2, 2)
                u = t - 2
                if 0 <= u < UN1:
                    pe.wait_ge(combined, u + 1)
                    b = take(("t1", u))
                    for kt in range(TT):
                        last = pe.transpose(psum[:, b, P * kt:P * kt + P], p1[:, u % 3, 0, P * kt:P * kt + P], ident[:, :])
                    last.then_inc(filled[b], 1)
                if t >= 5 and t % 2:
                    g = (t - 5) // 2
                    c = g // 4
                    if g == 0:
                        for kt in range(TT):
                            wait_emptied(pe, ("v1", kt))
                    wait_emptied(pe, ("t1", 2 * g))
                    wait_emptied(pe, ("t1", 2 * g + 1))
                    b = take(("o1", g))
                    for kt in range(TT):
                        last = three(psum[:, b, 0:2 * P], v1_hi[:, kt, P * c:P * c + P], v1_lo[:, kt, P * c:P * c + P],
                                     wt_hi[:, g % 2, kt, :], wt_lo[:, g % 2, kt, :], kt == 0, kt == TT - 1)
                    last.then_inc(filled[b], 1)
                if t == UN1:
                    pe.wait_ge(wpool_set, 1)
                    pe.wait_ge(pooled, 2)
                    for c2, src in enumerate((pool_d, pool_t)):
                        b = take(("pool", c2))
                        pe.matmul(psum[:, b, :], wpool_bd[:, c2, :], src[:, :], start=True, stop=True)\
                          .then_inc(filled[b], 1)

            b = take("sub_sum")
            pe.wait_ge(consts_set, N_CONSTS)
            for c in range(4):
                pe.wait_ge(o_squared, c + 1)
                for i in range(TT):
                    last = pe.matmul(psum[:, b, 8 * i + 2 * c:8 * i + 2 * c + 2], q1[:, c, P * i:P * i + P], mean_h,
                                     start=True, stop=True)
            last.then_inc(filled[b], 1)
            pe.wait_ge(sub_scaled, 1)
            for c in range(4):
                b = take(("sub", c))
                for i in range(TT):
                    for j in range(2):
                        at = 8 * i + 2 * c + j
                        last = pe.matmul(psum[DH * j:DH * j + DH, b, P * i:P * i + P],
                                         rsub[:, at:at + 1].to_broadcast([P, DH]), ident[:, :], start=True, stop=True)
                last.then_inc(filled[b], 1)

            ys = YS

            def out_proj(key, s0, xs, js, ready):
                def two(n0, i=None):
                    for n in (n0, n0 + 1):
                        await_slab(s0 + n, i, 2)
                        b = take((key,), n, i, 2)
                        chunk(psum[:, b, :], s0 + n, js, xs, ready).then_inc(w_used, 1)

                two(0)
                with repeat(pe, KD // 2 - 1, []) as i:
                    two(2, i)

            out_proj("out1", S_OUT1, [hs[k] for k in ys], ys, (h_ready, 8 * GEN["y"]))

            def token_sums(name, phase, kinds=1):
                pe.wait_ge(summed, SUM0 + SQUARES[phase] + KD * kinds)
                b = take(("sum", name))
                for m in range(kinds):
                    for i in range(TT):
                        last = pe.matmul(psum[:, b, 4 * m + i:4 * m + i + 1], acc[:, m, P * i:P * i + P], mean_d,
                                         start=True, stop=True)
                last.then_inc(filled[b], 1)

            def spread(key, col, ready):
                pe.wait_ge(cols_set, ready)
                b = take(key)
                for i in range(TT):
                    last = pe.matmul(psum[:, b, P * i:P * i + P], rcol[:, col + i:col + i + 1].to_broadcast([P, P]),
                                     ident[:, :], start=True, stop=True)
                last.then_inc(filled[b], 1)

            token_sums("ffn0", "out1")
            spread(("scale", "ffn0"), 4, 1)

            def ffn(f, between):
                s0 = S_GU[f]
                h0 = 8 * GEN[f"ffn{f}"]

                def pair(n, i=None):
                    for key, sl in (("gate", 0), ("up", 1)):
                        await_slab(s0 + 2 * n + sl, i, 2)
                        b = take((key, f), n, i)
                        chunk(psum[:, b, :], s0 + sl, range(KD), hs, (h_ready, h0)).then_inc(w_used, 1)
                        if n == 0 and sl == 0:
                            between()

                def down_pair(n0, i=None):
                    for n in (n0, n0 + 1):
                        for half in range(2):
                            s = S_DN[f] + 2 * n + half
                            await_slab(s, i, 4)
                            b = take(("down", f), n, i, 2) if half == 0 else bank_of(("down", f, n))
                            ks = range(HALF * half, HALF * half + HALF)
                            chunk(psum[:, b, :], s, range(HALF), [(hid_hi[:, k, :], hid_lo[:, k, :]) for k in ks],
                                  (hid_ready, KF * f + HALF * half), half == 0, half == 1).then_inc(w_used, 1)

                pair(0)
                pair(1)
                with repeat(pe, KF - 2, []) as i:
                    pair(2, i)
                down_pair(0)
                with repeat(pe, KD // 2 - 1, []) as i:
                    down_pair(2, i)

            ffn(0, lambda: None)

            def scale_ffn1():
                token_sums("ffn1", "down0", 2)
                spread(("scale", "ffn1"), 8, 2)
                spread(("scale2", "ffn1"), 4, 3)

            ffn(1, scale_ffn1)

            for s in range(S_PROJ2, S_PROJ2 + 4):
                await_slab(s)
                for i in range(TT):
                    b = take(("va", i)) if s == S_PROJ2 else i
                    for j in range(2):
                        k = 2 * (s - S_PROJ2) + j
                        pe.wait_ge(h_ready, 8 * GEN["mix2"] + k + 1)
                        ts = slice(P * i, P * i + P)
                        ws = slice(T * j, T * j + T)
                        last = three(psum[:, b, :], h_hi[:, k, ts], h_lo[:, k, ts], w_hi[:, s % 2, ws],
                                     w_lo[:, s % 2, ws], k == 0, k == KD - 1)
                last.then_inc(w_used, 1)
                if s == S_PROJ2:
                    token_sums("mix2", "down1")
                    spread(("scale", "mix2"), 4, 4)
            s = S_PROJ2 + 4
            await_slab(s)
            b = take("vb")
            for i in range(TT):
                for k in range(KD):
                    w = tile(s, k)
                    last = three(psum[:, b, P * i:P * i + P], h_hi[:, k, P * i:P * i + P], h_lo[:, k, P * i:P * i + P],
                                 *w, k == 0, k == KD - 1)
            last.then_inc(w_used, 1)

            def rope_turn(name, src, n):
                pe.wait_ge(roped, n)
                b = take(name)
                pe.matmul(psum[:, b, :], turn_m[:, :], src, start=True, stop=True).then_inc(filled[b], 1)

            whole("kb", S_PROJ2 + 5)
            for c in range(4):
                whole(("qb", c), S_QB + c)
                if c == 0:
                    rope_turn("kb_turn", kb[:, :], 1)
                else:
                    rope_turn(("qb_turn", c - 1), qb[:, c - 1, :], 1 + 2 * c)

            for t in range(UN2 + 4):
                if t == 0:
                    rope_turn(("qb_turn", 3), qb[:, 3, :], 9)
                if t < UN2:
                    windowed, c, j, i, head, kts = unit2(t)
                    r = DH * j
                    if t == 0:
                        pe.wait_ge(roped, 10)
                    if not windowed and t % 8 == 0:
                        wait_emptied(pe, ("slab", S_MIX2 + 2 * c))
                        wait_emptied(pe, ("slab", S_MIX2 + 2 * c + 1))
                    b = take(("s2", t))
                    ks = slice(P * kts[0], P * kts[-1] + P)
                    if windowed:
                        q_, k_ = qb[r:r + DH, c, P * i:P * i + P], kb[r:r + DH, ks]
                    else:
                        q_, k_ = qa[r:r + DH, c, P * i:P * i + P], ka[r:r + DH, c, ks]
                    pe.matmul(psum[:, b, 0:P * len(kts)], q_, k_, start=True, stop=True).then_inc(filled[b], 1)
                    part(S_MIX2 + t // 4, t % 4, 4)
                u = t - 2
                if 0 <= u < UN2:
                    kts = unit2(u)[5]
                    pe.wait_ge(combined2, u + 1)
                    b = take(("t2", u))
                    for n in range(len(kts)):
                        last = pe.transpose(psum[:, b, P * n:P * n + P], p2[:, u % 3, P * n:P * n + P], ident[:, :])
                    last.then_inc(filled[b], 1)
                if t >= 5 and t % 2:
                    g = (t - 5) // 2
                    windowed, c = unit2(2 * g)[0:2]
                    if g == 0:
                        wait_emptied(pe, "vb")
                        for kt in range(TT):
                            wait_emptied(pe, ("va", kt))
                    wait_emptied(pe, ("t2", 2 * g))
                    wait_emptied(pe, ("t2", 2 * g + 1))
                    b = take(("o2", g))
                    if not windowed:
                        sees = [(kt, 0, 2 * P) for kt in range(TT)]
                    elif g % 2 == 0:
                        sees = [(0, 0, 2 * P), (1, 0, 2 * P), (2, P, 2 * P)]
                    else:
                        sees = [(2, 0, 2 * P), (3, 0, 2 * P), (1, 0, P)]
                    for n, (kt, c0, c1) in enumerate(sees):
                        if windowed:
                            v_ = vb_hi[:, kt, :], vb_lo[:, kt, :]
                        else:
                            v_ = va_hi[:, kt, P * c:P * c + P], va_lo[:, kt, P * c:P * c + P]
                        last = three(psum[:, b, c0:c1], *v_, wt2_hi[:, g % 2, kt, c0:c1], wt2_lo[:, g % 2, kt, c0:c1],
                                     n == 0, n == len(sees) - 1)
                    last.then_inc(filled[b], 1)

            wait_emptied(pe, ("o2", UN2 // 2 - 1))
            ab = [(ya_hi[:, k, :], ya_lo[:, k, :]) for k in range(4)], [(yb_hi[:, k, :], yb_lo[:, k, :]) for k in range(4)]

            def gates(n, i=None):
                await_slab(S_MERGE + 2 * n, i, 2)
                b = take(("gb",), n, i)
                chunk(psum[:, b, :], S_MERGE, range(KD), hs).then_inc(w_used, 1)
                await_slab(S_MERGE + 2 * n + 1, i, 2)
                b = take(("a",), n, i)
                chunk(psum[:, b, :], S_MERGE + 1, range(0, 4), ab[0]).then_inc(filled[b], 1)
                b = take(("b",), n, i)
                chunk(psum[:, b, :], S_MERGE + 1, range(4, 8), ab[1]).then_inc(w_used, 1)

            gates(0)
            with repeat(pe, KD - 1, []) as i:
                gates(1, i)

            out_proj("out2", S_OUT2, [(m_hi[:, k, :], m_lo[:, k, :]) for k in range(KD)], range(KD), (m_ready, 0))

            def scale_ffn2():
                token_sums("ffn2", "out2")
                spread(("scale", "ffn2"), 4, 5)

            ffn(2, scale_ffn2)

            token_sums("last", "down2")
            for i in range(TT):
                for half in range(2):
                    b = take(("fin", i, half))
                    for k in range(4):
                        kk = 4 * half + k
                        pe.wait_ge(o_final, kk + 1)
                        last = pe.transpose(psum[:, b, P * k:P * k + P], o_scaled[:, kk, P * i:P * i + P], ident[:, :])
                    last.then_inc(filled[b], 1)

        @block.sync
        def _(sp):
            for i in range(TT):
                sp.dma_start(x_tok[:, i, :], ins["x"][0, P * i:P * i + P, :]).then_inc(x_landed, 16)
            ada = ins["w_ada"][0].rearrange("(k p) n -> p k n", p=P)
            for s in range(2):
                sp.dma_start(w_raw[:, s, 0:KD * P].rearrange("p (k n) -> p k n", k=KD),
                             ada[:, :, P * s:P * s + P]).then_inc(raw_landed[s], 16)
            with repeat(sp, N_ADA // 2 - 1, []) as i:
                for s in range(2):
                    src = ada[:, :, bass.ds(i * 2 * P + P * (s + 2), P)]
                    sp.wait_ge(ada_used, i * 2 + s + 1)
                    sp.dma_start(w_raw[:, s, 0:KD * P].rearrange("p (k n) -> p k n", k=KD), src)\
                      .then_inc(raw_landed[s], 16)

            def free(s, i=None, step=1):
                if s < 2:
                    sp.wait_ge(ada_used, N_ADA - 1 + s)
                else:
                    sp.wait_ge(w_ready, s - 1 if i is None else i * step + s - 1)

            def raw(s, j0=0, j1=KD, n=P):
                return w_raw[:, s % 2, j0 * P:j1 * P].rearrange("p (k n) -> p k n", n=n)

            def load(s, src, j0=0, j1=KD, n=P):
                sp.dma_start(raw(s, j0, j1, n), src).then_inc(raw_landed[s % 2], 16)

            w1 = ins["w_in"][0].rearrange("(k p) n -> p k n", p=P)
            AW, PW = 4 * P, 2 * P
            o_k, o_v, o_p, o_b, o_c, o_x = AW, 2 * AW, 3 * AW, 3 * AW + PW, 3 * AW + 2 * PW, 3 * AW + 3 * PW
            first = {"q": 0, "k": o_k, "u": o_p, "cg": o_c, "xc": o_x, "bg": o_b}
            for s in range(4):
                free(s)
                load(s, w1[:, 2 * s:2 * s + 2, o_v:o_v + T], n=T)
            for n, (kind, c) in enumerate([("q", 0), ("k", 0), *KINDS1]):
                free(S_Q0 + n)
                load(S_Q0 + n, w1[:, :, first[kind] + P * c:first[kind] + P * c + P])

            def columns(s0, w):
                src = w.rearrange("(k p) n -> p k n", p=P)
                with repeat(sp, KD // 2, []) as i:
                    for n in range(2):
                        free(s0 + n, i, 2)
                        load(s0 + n, src[:, :, bass.ds(i * 2 * P + P * n, P)])

            def ffn(f, w_gate, w_up, w_down):
                gate, up = (w.rearrange("(k p) n -> p k n", p=P) for w in (w_gate, w_up))
                with repeat(sp, KF, []) as i:
                    for n, src in enumerate((gate, up)):
                        free(S_GU[f] + n, i, 2)
                        load(S_GU[f] + n, src[:, :, bass.ds(i * P, P)])
                down = w_down.rearrange("(k p) n -> p k n", p=P)
                with repeat(sp, KD, []) as i:
                    for n in range(2):
                        free(S_DN[f] + n, i, 2)
                        load(S_DN[f] + n, down[:, HALF * n:HALF * n + HALF, bass.ds(i * P, P)], 0, HALF)

            columns(S_OUT1, ins["w_out"][0])
            wgu = ins["w_gate_up"][0]
            ffn(0, wgu[:, 0:FF], wgu[:, FF:2 * FF], ins["w_down"][0])
            ffn(1, ins["ffn1_w_gate_2"][0], ins["ffn1_w_up_2"][0], ins["ffn1_w_down_2"][0])

            w2 = ins["w_in_2"][0].rearrange("(k p) n -> p k n", p=P)
            o_qb, o_kb, o_vb, o_ga, o_gb = 3 * AW, 4 * AW, 4 * AW + P, 4 * AW + 2 * P, 4 * AW + 2 * P + D
            for s in range(4):
                free(S_PROJ2 + s)
                load(S_PROJ2 + s, w2[:, 2 * s:2 * s + 2, o_v:o_v + T], n=T)
            for n, at in enumerate((o_vb, o_kb)):
                free(S_PROJ2 + 4 + n)
                load(S_PROJ2 + 4 + n, w2[:, :, at:at + P])
            for c in range(4):
                free(S_QB + c)
                for j in range(2):
                    at = o_qb + DH * (c + 4 * j)
                    sp.dma_start(raw(S_QB + c)[:, :, DH * j:DH * j + DH], w2[:, :, at:at + DH])\
                      .then_inc(raw_landed[(S_QB + c) % 2], 16)
            for j in range(16):
                at = [P * (j // 2), o_k + P * (j // 2)][j % 2] if j < 8 else o_ga + P * (j - 8)
                free(S_MIX2 + j)
                load(S_MIX2 + j, w2[:, :, at:at + P])
            wa = ins["w_branch_a_2"][0].rearrange("(k p) n -> p k n", p=P)
            wb = ins["w_branch_b_2"][0].rearrange("(j k p) n -> p j k n", p=DH, k=4)
            for n in range(KD):
                s, cols = S_MERGE + 2 * n, slice(P * n, P * n + P)
                free(s)
                load(s, w2[:, :, o_gb + P * n:o_gb + P * n + P])
                free(s + 1)
                load(s + 1, wa[:, :, cols], 0, 4)
                for j in range(2):
                    sp.dma_start(raw(s + 1, 4, 8)[DH * j:DH * j + DH], wb[:, j, :, cols])\
                      .then_inc(raw_landed[1], 16)
            columns(S_OUT2, ins["w_out_2"][0])
            ffn(2, ins["ffn2_w_gate_2"][0], ins["ffn2_w_up_2"][0], ins["ffn2_w_down_2"][0])
            for i in range(TT):
                for side in tok_set:
                    sp.wait_ge(side, i + 1)
                sp.dma_start(out[0, P * i:P * i + P, :], o_tok[:, i, :]).then_inc(out_landed, 16)
            sp.wait_ge(out_landed, 16 * TT)

        @block.scalar
        def _(act):
            act.dma_start(ident[:, :], ins["k_ident"]).then_inc(const_landed, 16)
            act.dma_start(turn_m[:, :], ins["k_turn"]).then_inc(const_landed, 16)
            for name, n in VECTORS:
                r = ROW_OF[name]
                act.dma_start(rows[r:r + n, :], ins[name]).then_inc(rows_landed, 16)
            for n, name in enumerate(("lambda_q1", "lambda_q2", "lambda_k1", "lambda_k2")):
                act.dma_start(lamrow[:, DQ1 * n:DQ1 * n + DQ1], ins[name].to_broadcast([P, DQ1]))\
                   .then_inc(lam_landed, 16)
            act.dma_start(sink, ins["sink_logit_2"].to_broadcast([P, H])).then_inc(lam_landed, 16)
            act.dma_start(dist[:, :], ins["k_dist"]).then_inc(dist_landed, 16)
            for c in range(2):
                act.dma_start(count_sb[c], ins["k_count"][:, c, :]).then_inc(count_landed, 16)

            def split_high(s, i=None, step=1):
                act.wait_ge(raw_landed[s % 2], along(lambda m: landed_at[m], s, i, step))
                if s >= 2:
                    act.wait_ge(w_used, s - 1 if i is None else i * step + s - 1)
                n = tiles_of(s) * P
                act.activation(w_hi[:, s % 2, 0:n], w_raw[:, s % 2, 0:n], ACT.Identity).then_inc(w_high, 1)

            wait_emptied(act, "vectors")
            c0 = ROW_OF["c"]
            act.activation(cact[:, :], vcol[:, c0:c0 + KD], ACT.Silu).then_inc(cact_set, 1)
            act.wait_ge(x_landed, 16 * TT)
            for i in range(TT):
                if i:
                    act.wait_ge(x_rms, i)
                act.activation(junk[:, :], x_tok[:, i, :], ACT.Square, accum_out=rcol[:, i:i + 1]).then_inc(x_rms, 1)
            act.wait_ge(x_rms, TT)
            act.wait_ge(consts_set, N_CONSTS)
            act.activation(rcol[:, 4:8], rcol[:, 0:4], ACT.Sqrt, bias=eps, scale=1.0 / D).then_inc(x_root, 1)
            act.wait_ge(lam_prod, 1)
            act.activation(lamrow[:, 194:196], lamrow[:, 192:194], ACT.Exp).then_inc(lam_exp, 1)
            for k in range(KD):
                b = wait_filled(act, ("x", k))
                act.activation(x[:, k, :], psum[:, b, :], ACT.Identity).then_inc(emptied[b], 1)
            with repeat(act, N_ADA // 8, []) as i:
                for r in range(2):
                    b = wait_filled(act, ("ada",), r, i, 2)
                    act.activation(mod_row[0:1, bass.ds(i * 8 * P + 4 * P * r, 4 * P)], psum[0:1, b, :], ACT.Identity)\
                       .then_inc(emptied[b], 1)
            act.wait_ge(mod_set, 2)
            for k in range(KD):
                wait_emptied(act, ("xn", k))
                act.activation(h_hi[:, k, :], xn_t[:, k, :], ACT.Identity, bias=modc[:, SH1 + k:SH1 + k + 1],
                               scale=scale1[:, k:k + 1]).then_inc(h_high, 1)
                if k == 0:
                    split_high(0)

            def alibi_table(h):
                if h >= 2:
                    for m in range(2):
                        wait_emptied(act, ("s1", 4 * (h - 2) + 3, m))
                else:
                    act.wait_ge(dist_landed, 16)
                act.activation(alibi[:, h % 2, :], dist[:, :], ACT.Copy, scale=2.0 ** (-8.0 * (h + 1) / H))\
                   .then_inc(alibi_set, 1)

            alibi_table(0)
            for s in range(1, 5):
                split_high(s)
            for i in range(TT):
                b = wait_filled(act, ("v1", i))
                act.activation(v1_hi[:, i, :], psum[:, b, :], ACT.Identity).then_inc(v_high, 1)

            def keep_q1(name, c):
                b = wait_filled(act, name)
                act.activation(q1[:, c, :], psum[:, b, :], ACT.Copy, scale=-float(DQ1) ** -0.5).then_inc(emptied[b], 1)

            def keep_k1(name, c):
                b = wait_filled(act, name)
                act.activation(k1[:, c, :], psum[:, b, :], ACT.Copy).then_inc(emptied[b], 1)

            split_high(5)
            keep_q1(("slab", S_Q0), 0)
            split_high(6)
            keep_k1(("slab", S_Q0 + 1), 0)

            for t in range(UN1 + 5):
                if t < 2 * N_MIX1 and t % 2 == 0:
                    split_high(S_MIX1 + t // 2 + 1)
                if 2 <= t <= 2 * N_MIX1 and t % 2 == 0:
                    j = t // 2 - 1
                    kind, c = KINDS1[j]
                    name = ("slab", S_MIX1 + j)
                    if kind == "q":
                        keep_q1(name, c)
                    elif kind == "k":
                        keep_k1(name, c)
                    elif kind == "u":
                        if c == 0:
                            act.wait_ge(pads_set, 1)
                        else:
                            act.wait_ge(pooled, 1)
                        b = wait_filled(act, name)
                        act.activation(pool_u[:, 8:8 + T], psum[:, b, :], ACT.Copy).then_inc(emptied[b], 1)
                    elif kind == "cg":
                        b = wait_filled(act, name)
                        act.activation(conv_c[:, c, :], psum[:, b, :], ACT.Copy).then_inc(emptied[b], 1)
                u = t - 3
                if 0 <= u < UN1:
                    g = u // 2
                    if g >= 2:
                        wait_filled(act, ("o1", g - 2))
                    b = wait_filled(act, ("t1", u))
                    act.activation(wt_hi[:, g % 2, :, P * (u % 2):P * (u % 2) + P],
                                   psum[:, b, :].rearrange("p (k q) -> p k q", k=TT), ACT.Copy).then_inc(wt_high, 1)
                if t >= 6 and t % 2 == 0:
                    g = (t - 6) // 2
                    h, a = g // 2, g % 2
                    r = DH * (h % 2)
                    b = wait_filled(act, ("o1", g))
                    act.activation(o1[r:r + DH, h // 2, 2 * P * a:2 * P * a + 2 * P], psum[r:r + DH, b, 0:2 * P], ACT.Copy)\
                       .then_inc(emptied[b], 1)
                if t < UN1:
                    if t % 4 == 0 and t // 4 + 1 < H:
                        alibi_table(t // 4 + 1)
                    for m in range(2):
                        wait_emptied(act, ("s1", t, m))
                        act.activation(p1[:, t % 3, m, :], p1[:, t % 3, m, :], ACT.Exp, bias=stat[:, t % 3, m:m + 1],
                                       scale=-1.0, accum_out=stat[:, t % 3, 2 + m:3 + m]).then_inc(expd, 1)
                if t == UN1:
                    act.wait_ge(w_used, S_OUT1)
                    for c in range(2):
                        wait_emptied(act, ("slab", S_MIX1 + KINDS1.index(("bg", c))))
                    for c in (2, 3):
                        act.activation(h_hi[:, 4 + c, :], y_side[:, c, :], ACT.Identity).then_inc(h_high, 1)
            for c in range(2):
                b = wait_filled(act, ("pool", c))
                p0 = ROW_OF["pool_scale"] + c
                act.activation(y_side[:, c, :], psum[:, b, :], ACT.Copy, scale=vcol[:, p0:p0 + 1]).then_inc(emptied[b], 1)
            wait_emptied(act, ("o1", UN1 // 2 - 1))
            for c in range(4):
                act.activation(q1[:, c, :], o1[:, c, :], ACT.Square).then_inc(o_squared, 1)
            for c in range(2):
                wait_emptied(act, ("pool", c))
                act.activation(h_hi[:, 4 + c, :], y_side[:, c, :], ACT.Identity).then_inc(h_high, 1)
            b = wait_filled(act, "sub_sum")
            act.activation(rsub[:, :], psum[:, b, 0:32], ACT.Sqrt, bias=eps).then_inc(emptied[b], 1)
            for c in range(4):
                act.wait_ge(y_set, c + 1)
                act.activation(h_hi[:, c, :], k1[:, c, :], ACT.Identity).then_inc(h_high, 1)

            def wait_summed(phase, n, i, kinds=1):
                v = SUM0 + SQUARES[phase] + kinds * (n - 1)
                act.wait_ge(summed, v if i is None else i * 2 * kinds + v)

            def square(n, i, m=0, scale=1.0):
                act.activation(sq[:, n % 2, m, :], x[:, slot_of(n, i, 2), :], ACT.Square, scale=scale).then_inc(squared, 1)

            def col_of(name, n, i, step):
                return vcol[:, slot_of(ROW_OF[name] + n, i, step)]

            def wait_new(phase, n, i, step):
                v = NEW_X[phase] + n + 1
                act.wait_ge(x_new, v if i is None else i * step + v)

            def next_h(n, i, step, col):
                act.activation(h_hi[:, slot_of(n, i, step), :], x[:, slot_of(n, i, step), :], ACT.Identity, scale=col)\
                   .then_inc(h_high, 1)

            def out_chunks(phase, s0, col=None):
                with repeat(act, KD // 2, []) as i:
                    for n in range(2):
                        wait_summed(phase, n, i)
                        split_high(s0 + n + 1, i, 2)
                        wait_new(phase, n, i, 2)
                        if col is not None:
                            next_h(n, i, 2, col_of(col, n, i, 2))
                        square(n, i)

            out_chunks("out1", S_OUT1)

            def root(name):
                b = wait_filled(act, ("sum", name))
                act.activation(rcol[:, 0:4], psum[:, b, 0:4], ACT.Sqrt, bias=eps).then_inc(emptied[b], 1)

            root("ffn0")
            for k in range(KD):
                act.wait_ge(scaled_x, k + 1)
                act.activation(h_hi[:, k, :], hm[:, k % 2, :], ACT.Identity, bias=modc[:, SH2 + k:SH2 + k + 1],
                               scale=scale2[:, k:k + 1]).then_inc(h_high, 1)

            def ffn(f, between, down, last=False):
                s0 = S_GU[f]

                def pair(n, i=None):
                    split_high(s0 + 2 * n + 1, i, 2)
                    if n == 0:
                        between()
                    if f == 0:
                        b = wait_filled(act, ("gate", f), n, i)
                        act.activation(t_silu[:, :], psum[:, b, :], ACT.Silu).then_inc(gate_act, 1)
                    else:
                        v = KF * (f - 1) + n + 1
                        act.wait_ge(gate_scaled, v if i is None else i + v)
                        act.activation(t_silu[:, :], t_gate[:, :], ACT.Silu).then_inc(gate_act, 1)
                    split_high(s0 + 2 * n + 2, i, 2)
                    v = KF * f + n + 1
                    act.wait_ge(hid_set, v if i is None else i + v)
                    act.activation(hid_hi[:, slot_of(n, i), :], t_hid[:, :], ACT.Identity).then_inc(hid_high, 1)

                pair(0)
                with repeat(act, KF - 2, []) as i:
                    pair(1, i)
                pair(KF - 1)

                def down_pair(n0, i=None):
                    for n in (n0, n0 + 1):
                        s = S_DN[f] + 2 * n
                        wait_summed(f"down{f}", n, i, 2 if f == 0 else 1)
                        split_high(s + 1, i, 4)
                        if not (last and n == KD - 1):
                            split_high(s + 2, i, 4)
                        down(n, i)

                with repeat(act, KD // 2 - 1, []) as i:
                    down_pair(0, i)
                down_pair(KD - 2)

            def down0(n, i):
                wait_new("down0", n, i, 2)
                next_h(n, i, 2, gff[:, slot_of(n, i, 2)])
                square(n, i)
                square(n, i, 1, col_of("g_final", n, i, 2))

            ffn(0, lambda: None, down0)

            def scale_ffn1():
                b = wait_filled(act, ("sum", "ffn1"))
                act.activation(ms2[:, :], psum[:, b, 4:8], ACT.Identity)
                root("ffn1")
                act.wait_ge(root2, 1)
                act.activation(rcol[:, 0:4], rcol[:, 12:16], ACT.Sqrt, bias=eps).then_inc(root2, 1)

            def down1(n, i):
                wait_new("down1", n, i, 2)
                next_h(n, i, 2, col_of("mix_norm_2", n, i, 2))
                square(n, i)

            ffn(1, scale_ffn1, down1)

            split_high(S_PROJ2 + 1)
            root("mix2")
            for s in range(S_PROJ2 + 2, S_PROJ2 + 5):
                split_high(s)
            act.wait_ge(cols_set, 4)
            for i in range(TT):
                b = wait_filled(act, ("va", i))
                act.activation(va_hi[:, i, :], psum[:, b, :], ACT.Identity, scale=rcol[:, 4 + i:5 + i]).then_inc(v_high, 1)
            split_high(S_PROJ2 + 5)
            b = wait_filled(act, "vb")
            for i in range(TT):
                act.activation(vb_hi[:, i, :], psum[:, b, P * i:P * i + P], ACT.Identity, scale=rcol[:, 4 + i:5 + i])\
                   .then_inc(v_high, 1)
            for s in range(S_QB, S_QB + 5):
                split_high(s)

            for t in range(UN2 + 5):
                if t < UN2 and t % 4 == 0:
                    split_high(S_MIX2 + t // 4 + 1)
                u = t - 3
                if 0 <= u < UN2:
                    g, kts = u // 2, unit2(u)[5]
                    if g >= 2:
                        wait_filled(act, ("o2", g - 2))
                    b = wait_filled(act, ("t2", u))
                    act.activation(wt2_hi[:, g % 2, kts[0]:kts[-1] + 1, P * (u % 2):P * (u % 2) + P],
                                   psum[:, b, 0:P * len(kts)].rearrange("p (k q) -> p k q", q=P), ACT.Copy)\
                       .then_inc(wt2_high, 1)
                if t >= 6 and t % 2 == 0:
                    g = (t - 6) // 2
                    windowed, c, j = unit2(2 * g)[0:3]
                    r, a = DH * j, g % 2
                    y_ = yb_hi if windowed else ya_hi
                    b = wait_filled(act, ("o2", g))
                    act.activation(y_[r:r + DH, c, 2 * P * a:2 * P * a + 2 * P], psum[r:r + DH, b, 0:2 * P], ACT.Copy)\
                       .then_inc(y2_high, 1)
                if t < UN2:
                    windowed, _, _, _, head, kts = unit2(t)
                    w = P * len(kts)
                    act.wait_ge(scored2, t + 1)
                    act.activation(p2[:, t % 3, 0:w], p2[:, t % 3, 0:w], ACT.Exp, bias=stat[:, t % 3, 0:1],
                                   scale=-1.0, accum_out=stat[:, t % 3, 2:3]).then_inc(expd2, 1)
                    if windowed:
                        act.activation(stat[:, t % 3, 6:7], stat[:, t % 3, 0:1], ACT.Exp, bias=sink[:, head:head + 1])\
                           .then_inc(expd2, 1)

            with repeat(act, KD, []) as i:
                split_high(S_MERGE + 1, i, 2)
                act.wait_ge(sb_set, i + 1)
                act.activation(t_sb[:, :], t_sb[:, :], ACT.Sigmoid).then_inc(sa_set, 1)
                act.activation(t_sa[:, :], za[:, bass.ds(i, 1), :], ACT.Sigmoid).then_inc(sa_set, 1)
                split_high(S_MERGE + 2, i, 2)
                act.wait_ge(merged, i + 1)
                act.activation(m_hi[:, bass.ds(i, 1), :], t_m[:, :], ACT.Identity).then_inc(m_high, 1)

            out_chunks("out2", S_OUT2, "ffn2_norm_2")

            def down2(n, i):
                wait_new("down2", n, i, 2)
                square(n, i)
                act.activation(o_scaled[:, slot_of(n, i, 2), :], x[:, slot_of(n, i, 2), :], ACT.Identity,
                               scale=col_of("final_norm_2", n, i, 2)).then_inc(o_final, 1)

            ffn(2, lambda: root("ffn2"), down2, last=True)
            root("last")
            act.wait_ge(cols_set, 6)
            for i in range(TT):
                b = wait_filled(act, ("fin", i, 0))
                act.activation(o_tok[:, i, 0:T], psum[:, b, :], ACT.Identity, scale=rcol[:, 4 + i:5 + i])\
                   .then_inc(tok_set[0], 1)

        @block.vector
        def _(dve):
            steps = Count()

            def done(ins_):
                ins_.then_inc(dve_step, 1)
                steps.n += 1
                dve.wait_ge(dve_step, steps.now())

            for at, value in ((eps, EPS), (mean_d, 1.0 / D), (one, 1.0), (small[0:DH, 12:13], 1.0 / DH),
                              (small[DH:P, 12:13], 0.0), (small[0:DH, 13:14], 0.0), (small[DH:P, 13:14], 1.0 / DH)):
                dve.memset(at, value).then_inc(consts_set, 1)
            b = wait_filled(dve, "vectors")
            dve.tensor_copy(vcol[:, 0:N_ROWS], psum[:, b, 0:N_ROWS]).then_inc(emptied[b], 1)
            dve.wait_ge(lam_landed, 80)
            done(dve.tensor_tensor(lamrow[:, 128:192], lamrow[:, 0:64], lamrow[:, 64:128], ALU.mult))
            dve.tensor_reduce(lamrow[:, 192:194], lamrow[:, 128:192].rearrange("p (a d) -> p a d", a=2),
                              mybir.AxisListType.X, ALU.add).then_inc(lam_prod, 1)
            dve.tensor_scalar(neg_sink, sink, -1.0, None, ALU.mult).then_inc(lam_set, 1)
            dve.wait_ge(lam_exp, 1)
            dve.scalar_tensor_tensor(out=neg_lam, in0=lamrow[:, 195:196], scalar=-LAMBDA_INIT, in1=lamrow[:, 194:195],
                                     op0=ALU.add, op1=ALU.subtract).then_inc(lam_set, 1)
            dve.wait_ge(emptied[7], 1)
            s0 = ROW_OF["g_subln"]
            dve.tensor_scalar(sub8[:, :], vcol[:, s0:s0 + 4], 1.0 - LAMBDA_INIT, None, ALU.mult).then_inc(lam_set, 1)
            g0, f0 = ROW_OF["g_final"], ROW_OF["ffn1_norm_2"]
            dve.tensor_tensor(gff[:, :], vcol[:, g0:g0 + KD], vcol[:, f0:f0 + KD], ALU.mult).then_inc(lam_set, 1)
            dve.wait_ge(x_root, 1)
            done(dve.reciprocal(rcol[:, 8:12], rcol[:, 4:8]))
            for i in range(TT):
                dve.tensor_scalar(xn_tok[:, i, :], x_tok[:, i, :], rcol[:, 8 + i:9 + i], None, ALU.mult).then_inc(xn_set, 1)
            for k in range(KD):
                b = wait_filled(dve, ("xn", k))
                dve.tensor_copy(xn_t[:, k, :], psum[:, b, :]).then_inc(emptied[b], 1)
            b = wait_filled(dve, "mod")
            dve.tensor_tensor(modc[:, :], psum[:, b, 0:N_MOD], vcol[:, 0:N_MOD], ALU.add).then_inc(emptied[b], 1)
            wait_emptied(dve, "mod")
            for dst, at, g in ((scale1, SC1, "g_mix"), (scale2, SC2, "g_ffn")):
                dve.scalar_tensor_tensor(out=dst[:, :], in0=modc[:, at:at + KD], scalar=1.0,
                                         in1=vcol[:, ROW_OF[g]:ROW_OF[g] + KD], op0=ALU.add, op1=ALU.mult).then_inc(mod_set, 1)

            def split_low(s, i=None, step=1):
                dve.wait_ge(w_high, s + 1 if i is None else i * step + s + 1)
                n = tiles_of(s) * P
                dve.tensor_tensor(w_lo[:, s % 2, 0:n], w_raw[:, s % 2, 0:n], w_hi[:, s % 2, 0:n].bitcast(F32),
                                  ALU.subtract).then_inc(w_ready, 1)

            def low(dst, whole_, high, n, i=None, step=1):
                dve.wait_ge(h_high, n + 1 if i is None else i * step + n + 1)
                dve.tensor_tensor(dst, whole_, high.bitcast(F32), ALU.subtract).then_inc(h_ready, 1)

            dve.wait_ge(mod_set, 2)
            for k in range(KD):
                m = k % 2
                done(dve.tensor_scalar(hm[:, m, :], xn_t[:, k, :], scale1[:, k:k + 1], modc[:, SH1 + k:SH1 + k + 1],
                                       ALU.mult, ALU.add))
                low(h_lo[:, k, :], hm[:, m, :], h_hi[:, k, :], k)
                if k == 0:
                    split_low(0)
            for s in range(1, 5):
                split_low(s)
            for i in range(TT):
                b = bank[("v1", i)]
                dve.wait_ge(v_high, i + 1)
                dve.tensor_tensor(v1_lo[:, i, :], psum[:, b, :], v1_hi[:, i, :].bitcast(F32), ALU.subtract)\
                   .then_inc(emptied[b], 1)
            split_low(5)
            split_low(6)

            for t in range(UN1 + 5):
                if t < 2 * N_MIX1 and t % 2 == 0:
                    split_low(S_MIX1 + t // 2 + 1)
                if 2 <= t <= 2 * N_MIX1 and t % 2 == 0:
                    j = t // 2 - 1
                    kind, c = KINDS1[j]
                    if kind == "xc":
                        wait_emptied(dve, ("slab", S_MIX1 + KINDS1.index(("cg", c))))
                        dve.wait_ge(pads_set, 1)
                        b = wait_filled(dve, ("slab", S_MIX1 + j))
                        dve.tensor_tensor(conv_u[:, c, 1:T + 1], psum[:, b, :], conv_c[:, c, :], ALU.mult)\
                           .then_inc(emptied[b], 1)
                    elif kind == "bg":
                        dve.wait_ge(conved, c + 1)
                        b = wait_filled(dve, ("slab", S_MIX1 + j))
                        dve.tensor_tensor(y_side[:, 2 + c, :], psum[:, b, :], conv_c[:, c, :], ALU.mult)\
                           .then_inc(emptied[b], 1)
                u = t - 3
                if 0 <= u < UN1:
                    b = bank[("t1", u)]
                    at = slice(P * (u % 2), P * (u % 2) + P)
                    dve.wait_ge(wt_high, u + 1)
                    dve.tensor_tensor(wt_lo[:, u // 2 % 2, :, at], psum[:, b, :].rearrange("p (k q) -> p k q", k=TT),
                                      wt_hi[:, u // 2 % 2, :, at].bitcast(F32), ALU.subtract).then_inc(emptied[b], 1)
                if t < UN1:
                    h, i = t // 4, t % 4
                    if i == 0:
                        dve.wait_ge(alibi_set, h + 1)
                    if t >= 3:
                        wait_filled(dve, ("t1", t - 3))
                    for m in range(2):
                        b = wait_filled(dve, ("s1", t, m))
                        dve.tensor_tensor_reduce(p1[:, t % 3, m, :], psum[:, b, :],
                                                 alibi[:, h % 2, T - P - P * i:2 * T - P - P * i], 1.0, 3e38,
                                                 ALU.add, ALU.min, stat[:, t % 3, m:m + 1]).then_inc(emptied[b], 1)
                u = t - 1
                if 0 <= u < UN1:
                    st, n = stat[:, u % 3, :], u % 3
                    dve.wait_ge(expd, 2 * u + 2)
                    if u == 0:
                        dve.wait_ge(lam_set, 4)
                    done(dve.reciprocal(st[:, 4:6], st[:, 2:4]))
                    done(dve.tensor_scalar(p1[:, n, 1, :], p1[:, n, 1, :], st[:, 5:6], neg_lam, ALU.mult, ALU.mult))
                    dve.scalar_tensor_tensor(out=p1[:, n, 0, :], in0=p1[:, n, 0, :], scalar=st[:, 4:5],
                                             in1=p1[:, n, 1, :], op0=ALU.mult, op1=ALU.add).then_inc(combined, 1)
                if t == UN1:
                    for n, c in enumerate((2, 3)):
                        low(h_lo[:, 4 + c, :], y_side[:, c, :], h_hi[:, 4 + c, :], 8 + n)
            for c in range(2):
                low(h_lo[:, 4 + c, :], y_side[:, c, :], h_hi[:, 4 + c, :], 10 + c)
            wait_emptied(dve, "sub_sum")
            dve.reciprocal(rsub[:, :], rsub[:, :]).then_inc(sub_scaled, 1)
            wait_emptied(dve, ("o1", UN1 // 2 - 1))
            for c in range(4):
                b = wait_filled(dve, ("sub", c))
                dve.scalar_tensor_tensor(out=k1[:, c, :], in0=o1[:, c, :], scalar=sub8[:, c:c + 1], in1=psum[:, b, :],
                                         op0=ALU.mult, op1=ALU.mult).then_inc(y_set, 1)
                dve.wait_ge(y_set, c + 1)
                low(h_lo[:, c, :], k1[:, c, :], h_hi[:, c, :], 12 + c)

            def col_of(name, n, i, step):
                return vcol[:, slot_of(ROW_OF[name] + n, i, step)]

            def wait_new(phase, n, i, step):
                v = NEW_X[phase] + n + 1
                dve.wait_ge(x_new, v if i is None else i * step + v)

            def add_gated(name, phase, n, i, gt):
                b = wait_filled(dve, name, n, i, 2)
                at = slot_of(n, i, 2)
                dve.scalar_tensor_tensor(out=x[:, at, :], in0=psum[:, b:b + 1, :], scalar=modc[:, slot_of(gt + n, i, 2)],
                                         in1=x[:, at, :], op0=ALU.mult, op1=ALU.add).then_inc(x_new, 1)
                wait_new(phase, n, i, 2)

            def next_low(phase, gen, n, i, col):
                at = slot_of(n, i, 2)
                v = 8 * gen + n + 1
                dve.wait_ge(h_high, v if i is None else i * 2 + v)
                dve.scalar_tensor_tensor(out=h_lo[:, at, :], in0=x[:, at, :], scalar=col, in1=h_hi[:, at, :].bitcast(F32),
                                         op0=ALU.mult, op1=ALU.subtract).then_inc(h_ready, 1)

            with repeat(dve, KD // 2, []) as i:
                for n in range(2):
                    split_low(S_OUT1 + n + 1, i, 2)
                    add_gated(("out1",), "out1", n, i, GT1)

            def token_scale(name):
                wait_emptied(dve, ("sum", name))
                dve.reciprocal(rcol[:, 4:8], rcol[:, 0:4]).then_inc(cols_set, 1)

            def take_scale(name):
                b = wait_filled(dve, ("scale", name))
                dve.tensor_copy(rs[:, :], psum[:, b, :]).then_inc(scale_set, 1)
                dve.wait_ge(*free_at[("scale", name)])
                done(dve.tensor_scalar(rs_half[:, :], rs[:, :], 0.5, None, ALU.mult))

            token_scale("ffn0")
            take_scale("ffn0")
            for k in range(KD):
                if k >= 2:
                    dve.wait_ge(h_ready, 8 * GEN["ffn0"] + k - 1)
                dve.tensor_tensor(hm[:, k % 2, :], x[:, k, :], rs[:, :], ALU.mult).then_inc(scaled_x, 1)
                dve.wait_ge(scaled_x, k + 1)
                dve.wait_ge(h_high, 8 * GEN["ffn0"] + k + 1)
                done(dve.tensor_scalar(hm[:, k % 2, :], hm[:, k % 2, :], scale2[:, k:k + 1],
                                       modc[:, SH2 + k:SH2 + k + 1], ALU.mult, ALU.add))
                low(h_lo[:, k, :], hm[:, k % 2, :], h_hi[:, k, :], 8 * GEN["ffn0"] + k)

            def ffn(f, between, before_down, down, last=False):
                s0 = S_GU[f]

                def pair(n, i=None):
                    split_low(s0 + 2 * n + 1, i, 2)
                    if n == 0:
                        between()
                    if f:
                        b = wait_filled(dve, ("gate", f), n, i)
                        dve.tensor_tensor(t_gate[:, :], psum[:, b, :], rs[:, :], ALU.mult).then_inc(gate_scaled, 1)
                    split_low(s0 + 2 * n + 2, i, 2)
                    v = KF * f + n + 1
                    dve.wait_ge(gate_act, v if i is None else i + v)
                    b = wait_filled(dve, ("up", f), n, i)
                    dve.tensor_tensor(t_hid[:, :], psum[:, b, :], t_silu[:, :], ALU.mult).then_inc(hid_set, 1)
                    dve.wait_ge(hid_set, v if i is None else i + v)
                    dve.wait_ge(hid_high, v if i is None else i + v)
                    at = slot_of(n, i)
                    dve.tensor_tensor(hid_lo[:, at, :], t_hid[:, :], hid_hi[:, at, :].bitcast(F32), ALU.subtract)\
                       .then_inc(hid_ready, 1)

                pair(0)
                with repeat(dve, KF - 2, []) as i:
                    pair(1, i)
                pair(KF - 1)
                before_down()

                def down_pair(n0, i=None):
                    for n in (n0, n0 + 1):
                        s = S_DN[f] + 2 * n
                        split_low(s + 1, i, 4)
                        if not (last and n == KD - 1):
                            split_low(s + 2, i, 4)
                        down(n, i)

                with repeat(dve, KD // 2 - 1, []) as i:
                    down_pair(0, i)
                down_pair(KD - 2)

            def down0(n, i):
                add_gated(("down", 0), "down0", n, i, GT2)
                next_low("down0", GEN["ffn1"], n, i, gff[:, slot_of(n, i, 2)])

            ffn(0, lambda: None, lambda: None, down0)

            def scale_ffn1():
                wait_emptied(dve, ("sum", "ffn1"))
                dve.reciprocal(rcol[:, 8:12], rcol[:, 0:4]).then_inc(cols_set, 1)
                dve.wait_ge(cols_set, 2)
                done(dve.tensor_tensor(rcol[:, 12:16], ms2[:, :], rcol[:, 8:12], ALU.mult))
                dve.tensor_tensor(rcol[:, 12:16], rcol[:, 12:16], rcol[:, 8:12], ALU.mult).then_inc(root2, 1)
                dve.wait_ge(root2, 2)
                done(dve.reciprocal(rcol[:, 4:8], rcol[:, 0:4]))
                dve.tensor_tensor(rcol[:, 4:8], rcol[:, 4:8], rcol[:, 8:12], ALU.mult).then_inc(cols_set, 1)
                b = wait_filled(dve, ("scale", "ffn1"))
                dve.tensor_copy(rs_fin[:, :], psum[:, b, :]).then_inc(emptied[b], 1)
                b = wait_filled(dve, ("scale2", "ffn1"))
                dve.tensor_copy(rs[:, :], psum[:, b, :]).then_inc(scale_set, 1)
                dve.wait_ge(*free_at[("scale2", "ffn1")])
                done(dve.tensor_scalar(rs_half[:, :], rs[:, :], 0.5, None, ALU.mult))

            def final_norm():
                for k in range(KD):
                    last = dve.scalar_tensor_tensor(out=x[:, k, :], in0=x[:, k, :], scalar=vcol[:, g0 + k:g0 + k + 1],
                                                    in1=rs_fin[:, :], op0=ALU.mult, op1=ALU.mult)
                done(last)

            def add_scaled(name, phase, n, i):
                b = wait_filled(dve, name, n, i, 2)
                at = slot_of(n, i, 2)
                dve.tensor_tensor(t_gate[:, :], psum[:, b, :], rs_half[:, :], ALU.mult).then_inc(t_set, 1)
                v = {"down1": 0, "down2": KD}[phase] + n + 1
                dve.wait_ge(t_set, v if i is None else i * 2 + v)
                dve.tensor_tensor(x[:, at, :], t_gate[:, :], x[:, at, :], ALU.add).then_inc(x_new, 1)
                wait_new(phase, n, i, 2)

            def down1(n, i):
                add_scaled(("down", 1), "down1", n, i)
                next_low("down1", GEN["mix2"], n, i, col_of("mix_norm_2", n, i, 2))

            ffn(1, scale_ffn1, final_norm, down1)

            split_low(S_PROJ2 + 1)
            token_scale("mix2")
            take_scale("mix2")
            for s in range(S_PROJ2 + 2, S_PROJ2 + 5):
                split_low(s)
            for i in range(TT):
                b = bank[("va", i)]
                dve.wait_ge(v_high, TT + i + 1)
                dve.scalar_tensor_tensor(out=va_lo[:, i, :], in0=psum[:, b, :], scalar=rcol[:, 4 + i:5 + i],
                                         in1=va_hi[:, i, :].bitcast(F32), op0=ALU.mult, op1=ALU.subtract)\
                   .then_inc(emptied[b], 1)
            split_low(S_PROJ2 + 5)
            b = bank["vb"]
            dve.wait_ge(v_high, 3 * TT)
            for i in range(TT):
                last = dve.scalar_tensor_tensor(out=vb_lo[:, i, :], in0=psum[:, b, P * i:P * i + P],
                                                scalar=rcol[:, 4 + i:5 + i], in1=vb_hi[:, i, :].bitcast(F32),
                                                op0=ALU.mult, op1=ALU.subtract)
            last.then_inc(emptied[b], 1)

            def embed(name, dst):
                b = wait_filled(dve, name)
                dve.tensor_tensor(z_t, psum[:, b, :], sin_sb[:, :], ALU.mult).then_inc(emptied[b], 1)
                done(dve.tensor_tensor(z_c, dst, cos_sb[:, :], ALU.mult))
                wait_emptied(dve, name)
                dve.tensor_tensor(dst, z_t, z_c, ALU.add).then_inc(roped, 1)

            split_low(S_QB)
            dve.wait_ge(table_landed, 64)
            b = wait_filled(dve, "kb")
            dve.tensor_tensor(kb[:, :], psum[:, b, :], rs[:, :], ALU.mult).then_inc(roped, 1)
            dve.wait_ge(roped, 1)
            for c in range(4):
                split_low(S_QB + c + 1)
                if c == 0:
                    embed("kb_turn", kb[:, :])
                else:
                    embed(("qb_turn", c - 1), qb[:, c - 1, :])
                b = wait_filled(dve, ("qb", c))
                dve.scalar_tensor_tensor(out=qb[:, c, :], in0=psum[:, b, :], scalar=-float(DH) ** -0.5, in1=rs[:, :],
                                         op0=ALU.mult, op1=ALU.mult).then_inc(roped, 1)
                dve.wait_ge(roped, 3 + 2 * c)
            embed(("qb_turn", 3), qb[:, 3, :])

            for t in range(UN2 + 5):
                if t < UN2 and t % 4 == 0:
                    split_low(S_MIX2 + t // 4 + 1)
                if 4 <= t <= UN2 and t % 4 == 0:
                    j = t // 4 - 1
                    b = wait_filled(dve, ("slab", S_MIX2 + j))
                    if j < 8 and j % 2 == 0:
                        dve.scalar_tensor_tensor(out=qa[:, j // 2, :], in0=psum[:, b, :], scalar=-float(DH) ** -0.5,
                                                 in1=rs[:, :], op0=ALU.mult, op1=ALU.mult).then_inc(emptied[b], 1)
                    else:
                        dst = ka[:, j // 2, :] if j < 8 else za[:, j - 8, :]
                        dve.tensor_tensor(dst, psum[:, b, :], rs[:, :], ALU.mult).then_inc(emptied[b], 1)
                u = t - 3
                if 0 <= u < UN2:
                    kts = unit2(u)[5]
                    b = bank[("t2", u)]
                    at = (slice(None), u // 2 % 2, slice(kts[0], kts[-1] + 1), slice(P * (u % 2), P * (u % 2) + P))
                    dve.wait_ge(wt2_high, u + 1)
                    dve.tensor_tensor(wt2_lo[at], psum[:, b, 0:P * len(kts)].rearrange("p (k q) -> p k q", q=P),
                                      wt2_hi[at].bitcast(F32), ALU.subtract).then_inc(emptied[b], 1)
                if t >= 6 and t % 2 == 0:
                    g = (t - 6) // 2
                    windowed, c, j = unit2(2 * g)[0:3]
                    r, a = DH * j, g % 2
                    y_, yl = (yb_hi, yb_lo) if windowed else (ya_hi, ya_lo)
                    at = (slice(r, r + DH), c, slice(2 * P * a, 2 * P * a + 2 * P))
                    b = bank[("o2", g)]
                    dve.wait_ge(y2_high, g + 1)
                    dve.tensor_tensor(yl[at], psum[r:r + DH, b, 0:2 * P], y_[at].bitcast(F32), ALU.subtract)\
                       .then_inc(emptied[b], 1)
                if t < UN2:
                    windowed, c, j, i, head, kts = unit2(t)
                    w, st = P * len(kts), stat[:, t % 3, :]
                    if t >= 3:
                        wait_filled(dve, ("t2", t - 3))
                    b = wait_filled(dve, ("s2", t))
                    if windowed:
                        off = P * (kts[0] - (i - 1))
                        bias = band[:, off:off + w]
                    else:
                        if i == 0:
                            dve.wait_ge(near_set, head + 1)
                        at = DR // 2 - 1 - 2 * i
                        bias = near[:, head % 2, at:at + NEAR_ROWS, :].rearrange("p a b -> p (a b)")
                    dve.tensor_tensor_reduce(p2[:, t % 3, 0:w], psum[:, b, 0:w], bias, 1.0, 3e38, ALU.add, ALU.min,
                                             st[:, 0:1]).then_inc(free_at[("s2", t)][0], 1)
                    if windowed:
                        wait_emptied(dve, ("s2", t))
                        dve.tensor_scalar(st[:, 0:1], st[:, 0:1], neg_sink[:, head:head + 1], None, ALU.min)\
                           .then_inc(scored2, 1)
                u = t - 1
                if 0 <= u < UN2:
                    windowed, w, st = unit2(u)[0], P * len(unit2(u)[5]), stat[:, u % 3, :]
                    dve.wait_ge(expd2, exps2(u))
                    if windowed:
                        done(dve.tensor_tensor(st[:, 2:3], st[:, 2:3], st[:, 6:7], ALU.add))
                    done(dve.reciprocal(st[:, 4:5], st[:, 2:3]))
                    dve.tensor_scalar(p2[:, u % 3, 0:w], p2[:, u % 3, 0:w], st[:, 4:5], None, ALU.mult)\
                       .then_inc(combined2, 1)

            with repeat(dve, KD, []) as i:
                split_low(S_MERGE + 1, i, 2)
                b = wait_filled(dve, ("gb",), 0, i)
                dve.tensor_tensor(t_sb[:, :], psum[:, b, :], rs[:, :], ALU.mult).then_inc(sb_set, 1)
                split_low(S_MERGE + 2, i, 2)
                dve.wait_ge(sa_set, i * 2 + 2)
                for key, t_ in (("a", t_sa), ("b", t_sb)):
                    b = wait_filled(dve, (key,), 0, i)
                    dve.tensor_tensor(t_[:, :], psum[:, b, :], t_[:, :], ALU.mult).then_inc(branch_set, 1)
                dve.wait_ge(branch_set, i * 2 + 2)
                dve.tensor_tensor(t_m[:, :], t_sa[:, :], t_sb[:, :], ALU.add).then_inc(merged, 1)
                dve.wait_ge(merged, i + 1)
                dve.wait_ge(m_high, i + 1)
                dve.tensor_tensor(m_lo[:, bass.ds(i, 1), :], t_m[:, :], m_hi[:, bass.ds(i, 1), :].bitcast(F32),
                                  ALU.subtract).then_inc(m_ready, 1)

            with repeat(dve, KD // 2, []) as i:
                for n in range(2):
                    split_low(S_OUT2 + n + 1, i, 2)
                    b = wait_filled(dve, ("out2",), n, i, 2)
                    at = slot_of(n, i, 2)
                    dve.tensor_tensor(x[:, at, :], psum[:, b:b + 1, :], x[:, at, :], ALU.add).then_inc(x_new, 1)
                    wait_new("out2", n, i, 2)
                    next_low("out2", GEN["ffn2"], n, i, col_of("ffn2_norm_2", n, i, 2))

            def scale_ffn2():
                token_scale("ffn2")
                take_scale("ffn2")

            ffn(2, scale_ffn2, lambda: None, lambda n, i: add_scaled(("down", 2), "down2", n, i), last=True)
            token_scale("last")
            dve.wait_ge(cols_set, 6)
            for i in range(TT):
                b = wait_filled(dve, ("fin", i, 1))
                dve.tensor_scalar(o_tok[:, i, T:D], psum[:, b, :], rcol[:, 4 + i:5 + i], None, ALU.mult)\
                   .then_inc(tok_set[1], 1)

        @block.gpsimd
        def _(pool):
            steps = Count()

            def done(ins_):
                ins_.then_inc(pool_step, 1)
                steps.n += 1
                pool.wait_ge(pool_step, steps.now())

            pool.dma_start(rpb_rows, ins["rpb"].unsqueeze(0).to_broadcast([GRID, n_rpb])).then_inc(rpb_copied, 16)
            pool.wait_ge(h_ready, KD)
            done(pool.memset(wpool_bd[:, :, :], 0.0))
            for g in range(4):
                r = DH * (g % 2)
                pool.dma_start(wpool_bd[r:r + DH, g // 2, r:r + DH], ins["w_pool"][0, g]).then_inc(wpool_landed, 16)
            done(pool.memset(pool_u[:, :], 0.0))
            done(pool.memset(conv_u[:, :, :], 0.0))
            pool.memset(pool_s[:, :, 0:1], 0.0).then_inc(pads_set, 1)
            pool.wait_ge(wpool_landed, 64)
            pool.memset(small[:, 24:25], 0.0).then_inc(wpool_set, 1)
            pool.wait_ge(count_landed, 32)

            def window_sum(dst, src, reach, lo, hi):
                left, right = (1, 0) if reach == 0 else (reach, reach)
                done(pool.tensor_tensor(dst[:, lo:hi], src[:, lo - left:hi - left], src[:, lo + right:hi + right], ALU.add))

            for c, dst in enumerate((pool_d, pool_t)):
                wait_emptied(pool, ("slab", S_MIX1 + KINDS1.index(("u", c))))
                sa_, sb_ = pool_s[:, 0, :], pool_s[:, 1, :]
                window_sum(sa_, pool_u, 0, 1, T + 15)
                window_sum(sb_, sa_, 1, 2, T + 14)
                if c == 1:
                    window_sum(sa_, sb_, 2, 4, T + 12)
                    window_sum(sb_, sa_, 4, 8, T + 8)
                for half in range(2):
                    r = slice(DH * half, DH * half + DH)
                    done(pool.tensor_tensor(dst[r, :], pool_s[r, half, 8:8 + T], count_sb[c][r, :], ALU.mult))
                pool.tensor_tensor(dst[:, :], dst[:, :], pool_u[:, 8:8 + T], ALU.subtract).then_inc(pooled, 1)
                pool.wait_ge(pooled, c + 1)
            w0 = ROW_OF["conv_w"]
            for c in range(2):
                wait_emptied(pool, ("slab", S_MIX1 + KINDS1.index(("xc", c))))
                taps = [vcol[:, w0 + 2 * j + c:w0 + 2 * j + c + 1] for j in range(3)]
                done(pool.tensor_scalar(conv_c[:, c, :], conv_u[:, c, 0:T], taps[0], None, ALU.mult))
                for j in (1, 2):
                    done(pool.tensor_scalar(pool_s[:, 0, 0:T], conv_u[:, c, j:T + j], taps[j], None, ALU.mult))
                    last = pool.tensor_tensor(conv_c[:, c, :], conv_c[:, c, :], pool_s[:, 0, 0:T], ALU.add)
                    if j == 1:
                        done(last)
                last.then_inc(conved, 1)
                pool.wait_ge(conved, c + 1)

            def sums(phase, clear, kinds=1):
                if clear:
                    wait_filled(pool, ("sum", clear))
                    done(pool.memset(acc[:, 0:kinds, :], 0.0))
                else:
                    pool.memset(acc[:, 0:kinds, :], 0.0).then_inc(summed, SUM0)
                    pool.wait_ge(summed, SUM0)
                with repeat(pool, KD // 2, []) as i:
                    for n in range(2):
                        for m in range(kinds):
                            v = SQUARES[phase] + kinds * n + m + 1
                            pool.wait_ge(squared, i * 2 * kinds + v)
                            pool.tensor_tensor(acc[:, m, :], acc[:, m, :], sq[:, n, m, :], ALU.add).then_inc(summed, 1)
                            pool.wait_ge(summed, i * 2 * kinds + v + SUM0)

            sums("out1", None)
            sums("down0", "ffn0", 2)
            pool.wait_ge(hid_ready, 2 * KF)
            for dst, name in ((sin_sb, "k_sin"), (band, "k_band"), (near_mask, "k_near")):
                pool.dma_start(dst[:, :], ins[name]).then_inc(table_landed, 16)
            sums("down1", "ffn1")
            pool.wait_ge(x_new, NEW_X["down1"] + KD)
            pool.dma_start(cos_sb[:, :], ins["k_cos"]).then_inc(table_landed, 16)

            def near_load(h):
                for odd in range(2):
                    at = PAD + h * DR * DC + (1 - odd) * DC + NEAR_COLS - 1
                    src = bass.AP(tensor=rpb_rows.tensor, offset=at, ap=[[n_rpb - 1, GRID], [DC, DR - 1], [1, GRID]])
                    pool.dma_start(near[GRID * odd:GRID * odd + GRID, h % 2, :, :], src).then_inc(near_landed[h % 2], 16)

            pool.wait_ge(table_landed, 64)
            pool.wait_ge(rpb_copied, 16)
            near_load(0)
            near_load(1)
            for h in range(H):
                pool.wait_ge(near_landed[h % 2], 32 * (h // 2 + 1))
                pool.tensor_tensor(near[:, h % 2, :, :], near_mask[:, :].unsqueeze(1).to_broadcast([P, DR - 1, GRID]),
                                   near[:, h % 2, :, :], ALU.subtract).then_inc(near_set, 1)
                if h + 2 < H:
                    wait_emptied(pool, ("s2", UN2 // 2 + 4 * h + 3))
                    near_load(h + 2)
            sums("out2", "mix2")
            sums("down2", "ffn2")


def kernel(**inputs):
    from concourse import bacc
    from concourse.bass_utils import run_bass_kernel_spmd

    vectors = {name for name, _ in VECTORS}
    arrays = {}
    for name, a in inputs.items():
        a = np.asarray(a)
        if name == "c" or name in vectors:
            a = a.reshape(-1, P)
        elif name == "na_rpb_2":
            name, a = "rpb", np.concatenate([np.zeros(PAD, a.dtype), a.reshape(-1), np.zeros(GRID + DC, a.dtype)])
        arrays[name] = np.ascontiguousarray(a)
    arrays.update(constants())
    nc = bacc.Bacc("TRN2", target_bir_lowering=False, num_devices=1)
    named = {f"in_{k}": v for k, v in arrays.items()}
    ins = {k[3:]: nc.dram_tensor(k, v.shape, mybir.dt.from_np(v.dtype), kind="ExternalInput").ap()
           for k, v in named.items()}
    out = nc.dram_tensor("out_0", (1, T, D), F32, kind="ExternalOutput").ap()
    program(nc, ins, out)
    r = run_bass_kernel_spmd(nc, [named], core_ids=[0])
    return r.results[0]["out_0"]
```

```python
from contextlib import ExitStack, contextmanager

import concourse.bass as bass
import numpy as np
from concourse import mybir

P = 128
T = 512
D = 1024
KD = D // P
TT = T // P
FF = 2816
KF = FF // P
HALF = KF // 2
H = 8
DQ1 = 32
DH = 64
GRID = 64
NEAR_ROWS, NEAR_COLS = 8, 16
DR = 2 * NEAR_ROWS - 1
DC = 2 * NEAR_COLS - 1
WIN = 128
EPS = 1e-6
FAR = 1e30
PAD = GRID - NEAR_COLS
LAMBDA_INIT = 0.2

F32 = mybir.dt.float32
F32R = mybir.dt.float32r
ALU = mybir.AluOpType
ACT = mybir.ActivationFunctionType
BYTES = 4

VECTORS = [("b_ada", 48), ("c", 8), ("g_mix", 8), ("g_subln", 4), ("pool_scale", 2), ("conv_w", 6),
           ("g_ffn", 8), ("g_final", 8), ("ffn1_norm_2", 8), ("mix_norm_2", 8), ("ffn2_norm_2", 8),
           ("final_norm_2", 8)]
ROW_OF, _at = {}, 0
for _name, _rows in VECTORS:
    ROW_OF[_name] = _at
    _at += _rows
N_ROWS = _at

SH1, SC1, GT1, SH2, SC2, GT2 = (KD * j for j in range(6))
N_MOD = 6 * KD


def constants():
    p = np.arange(P)
    out = {"k_ident": np.eye(P, dtype=np.float32)}
    f = p % DH
    turn = np.zeros((P, P), np.float32)
    turn[p, np.where(f < DH // 2, p + DH // 2, p - DH // 2)] = 1.0
    out["k_turn"] = turn
    out["k_dist"] = np.abs(p[:, None] - np.arange(2 * T - P)[None, :] + T - P).astype(np.float32)
    out["k_band"] = np.where(np.abs(p[:, None] + P - np.arange(3 * P)[None, :]) > WIN, FAR, 0.0).astype(np.float32)
    col = p % GRID
    start = np.clip(col - NEAR_COLS // 2, 0, GRID - NEAR_COLS)
    key = np.arange(GRID)[None, :]
    inside = (key >= start[:, None]) & (key < start[:, None] + NEAR_COLS)
    out["k_near"] = np.where(inside, 0.0, FAR).astype(np.float32)
    half = DH // 2
    inv = np.float32(10000.0) ** (-np.arange(half, dtype=np.float32) / np.float32(half))
    ang = np.arange(T, dtype=np.float32)[None, :] * inv[(f % half)][:, None]
    out["k_cos"] = np.cos(ang).astype(np.float32)
    out["k_sin"] = (np.sin(ang) * np.where(f < half, -1.0, 1.0)[:, None]).astype(np.float32)
    t = np.arange(T)
    rows = []
    for w in (2, 4, 8, 16):
        n = np.clip(t + w - w // 2, 0, T) - np.clip(t - w // 2, 0, T)
        rows.append(np.repeat((1.0 / n)[None], DH, 0))
    out["k_count"] = np.stack([np.concatenate(rows[0:2]), np.concatenate(rows[2:4])], 1).astype(np.float32)
    return out


class Count:

    def __init__(self):
        self.n, self.i, self.slope = 0, None, 0

    def now(self, ahead=0):
        v = self.n + ahead
        return v if self.i is None else self.i * self.slope + v


@contextmanager
def repeat(eng, times, slopes):
    before = [(c, c.n, s) for c, s in slopes]
    with eng.Fori(0, times) as i:
        for c, _, s in before:
            c.i, c.slope = i, s
        yield i
    for c, n, s in before:
        assert c.n - n == s, (c.n - n, s)
        c.n, c.i = n + s * times, None


def program(nc, ins, out):
    ctx = ExitStack()
    with ctx:
        def sem(name):
            return ctx.enter_context(nc.semaphore(name))

        BASE = 16512
        END = nc.sbuf_usable_end
        area = {"at": BASE}

        def place(name, shape, dt=F32, at=None):
            size = int(np.prod(shape[1:])) * BYTES
            size += -size % 32
            where = area["at"] if at is None else at
            if at is None:
                area["at"] += size
                assert area["at"] <= END, (name, area["at"], END)
            return nc.alloc_sbuf_tensor_at(name, list(shape), dt, offset=where)

        def region(start, limit, items):
            at, got = start, []
            for name, shape, dt in items:
                size = int(np.prod(shape[1:])) * BYTES
                got.append(place(name, shape, dt, at))
                at += size + (-size % 32)
                assert at <= limit, (name, at, limit)
            return got, at

        x = place("x_res", [P, KD, T])
        x_tok = place("x_tok", [P, TT, D], at=area["at"])
        o_scaled = place("o_scaled", [P, KD, T], at=area["at"])
        h_hi = place("h_hi", [P, KD, T], F32R)
        xn_tok = place("xn_tok", [P, TT, D], at=area["at"])
        h_lo = place("h_lo", [P, KD, T], F32R)
        w_raw = place("w_raw", [P, 2, HALF * P])
        w_hi = place("w_hi", [P, 2, HALF * P], F32R)
        w_lo = place("w_lo", [P, 2, HALF * P], F32R)
        ident = place("ident", [P, P])
        turn_m = place("turn_m", [P, P])
        rows = place("rows", [P, P])
        vcol = place("vcol", [P, P])
        modc = place("modc", [P, N_MOD])
        scale1 = place("scale1", [P, KD])
        scale2 = place("scale2", [P, KD])
        gff = place("gff", [P, KD])
        cact = place("cact", [P, KD])
        small = place("small", [P, 32])
        rcol = place("rcol", [P, 16])
        lamrow = place("lamrow", [P, 200])
        stat = place("stat", [P, 3, 8])
        rsub = place("rsub", [P, 32])
        ms2 = place("ms2", [P, 4])
        sub8 = place("sub8", [P, 4])
        acc = place("acc", [P, 2, T])
        sq = place("sq", [P, 2, 2, T])
        rs = place("rs", [P, T])
        rs_half = place("rs_half", [P, T])
        rs_fin = place("rs_fin", [P, T])
        OVER = area["at"]
        BIG_SIZE = 2 * KF * T * BYTES
        BIG = END - BIG_SIZE
        BIG -= BIG % 32
        BIG_END = BIG + BIG_SIZE

        eps = small[:, 0:1]
        mean_d = small[:, 1:2]
        one_col = small[:, 2:3]
        neg_lam = small[:, 3:4]
        sink = small[:, 4:12]
        neg_sink = small[:, 14:22]
        mean_h = small[:, 12:14]

        (hid_hi, hid_lo), _ = region(BIG, BIG_END, [("hid_hi", [P, KF, T], F32R), ("hid_lo", [P, KF, T], F32R)])
        (t_gate, t_silu, t_hid), _ = region(OVER, BIG, [(n, [P, T], F32) for n in ("t_gate", "t_silu", "t_hid")])
        (x_scaled, h_full), _ = region(OVER + 3 * T * BYTES, BIG, [(n, [P, 2, T], F32) for n in ("x_scaled", "h_full")])
        (xn_t, ada_w), _ = region(BIG, BIG_END, [("xn_t", [P, KD, T], F32), ("ada_w", [P, 4, KD * T], F32)])
        ada_row = sq[:, :, :, :].rearrange("p a b t -> p a (b t)")
        mod_acc = acc[:, :, :].rearrange("p a t -> p (a t)")
        (junk, hm, mod_row, first_acc), _ = region(OVER, BIG, [
            ("junk", [P, D], F32), ("hm", [P, 2, T], F32), ("mod_row", [1, D], F32), ("first_acc", [P, D], F32)])
        (q1, k1, v1_hi, v1_lo, wt_hi, wt_lo, o1, p1, alibi, dist), at1 = region(BIG, BIG_END, [
            ("q1", [P, 4, T], F32), ("k1", [P, 4, T], F32), ("v1_hi", [P, TT, T], F32R),
            ("v1_lo", [P, TT, T], F32R), ("wt_hi", [P, 2, TT, 2 * P], F32R),
            ("wt_lo", [P, 2, TT, 2 * P], F32R), ("o1", [P, 4, T], F32), ("p1", [P, 3, 2, T], F32),
            ("alibi", [P, 2, 2 * T - P], F32), ("dist", [P, 2 * T - P], F32)])
        y_side = place("y_side", [P, 4, T], F32, at1)
        assert at1 + 4 * T * BYTES <= BIG_END
        (pool_u, pool_s, pool_d, conv_c, conv_u, wpool_bd), _ = region(OVER, BIG, [
            ("pool_u", [P, T + 16], F32), ("pool_s", [P, 2, T + 16], F32), ("pool_d", [P, T], F32),
            ("conv_c", [P, 2, T], F32), ("conv_u", [P, 2, T + 2], F32), ("wpool_bd", [P, 2, P], F32)])
        pool_t = rs
        count_sb = rs_half[:, :], rs_fin[:, :]
        z_t, z_c = sq[:, 0, 0, :], sq[:, 0, 1, :]
        (cos_sb, sin_sb, band, near_mask, yb_lo, kb), BIG2 = region(OVER, BIG, [
            ("cos_sb", [P, T], F32), ("sin_sb", [P, T], F32),
            ("band", [P, 3 * P], F32), ("near_mask", [P, GRID], F32), ("yb_lo", [P, 4, T], F32R),
            ("kb", [P, T], F32)])
        (qa, ka, va_hi, va_lo, qb, vb_hi, vb_lo, near, wt2_hi, wt2_lo, za, p2), _ = region(BIG2, END, [
            ("qa", [P, 4, T], F32), ("ka", [P, 4, T], F32), ("va_hi", [P, TT, T], F32R),
            ("va_lo", [P, TT, T], F32R), ("qb", [P, 4, T], F32), ("vb_hi", [P, TT, P], F32R),
            ("vb_lo", [P, TT, P], F32R), ("near", [P, 2, DR - 1, GRID], F32),
            ("wt2_hi", [P, 2, TT, 2 * P], F32R), ("wt2_lo", [P, 2, TT, 2 * P], F32R),
            ("za", [P, KD, T], F32), ("p2", [P, 3, T], F32)])
        size4 = 4 * T * BYTES
        ya_hi = place("ya_hi", [P, 4, T], F32R, BIG2)
        ya_lo = place("ya_lo", [P, 4, T], F32R, BIG2 + size4)
        m_hi = place("m_hi", [P, KD, T], F32R, BIG2 + 2 * size4)
        yb_hi = place("yb_hi", [P, 4, T], F32R, BIG2 + 4 * size4)
        WT_AT = BIG2 + 5 * size4 + 2 * TT * P * BYTES + 2 * (DR - 1) * GRID * BYTES
        m_lo = place("m_lo", [P, KD, T], F32R, WT_AT)
        (t_sa, t_sb, t_m), _ = region(WT_AT + 2 * size4 + KD * T * BYTES, END, [
            (n, [P, T], F32) for n in ("t_sa", "t_sb", "t_m")])
        o_tok = place("o_tok", [P, TT, D], at=BIG)
        psum = ctx.enter_context(nc.psum_tensor("psum", [P, 8, T], F32))
        n_rpb = ins["rpb"].shape[0]
        rpb_rows = nc.dram_tensor("rpb_rows", (GRID, n_rpb), F32, kind="Internal").ap()

        S_V, S_Q0, S_MIX1 = 0, 4, 6
        S_OUT1 = 20
        S_GU = [28, 88, 198]
        S_DN = [72, 132, 242]
        S_PROJ2, S_QB, S_MIX2 = 148, 154, 158
        S_MERGE, S_OUT2 = 174, 190
        N_SLABS = 258
        MOD_STEP = {8: SH2 // KD, 20: SC2 // KD}
        UN1, UN2 = 32, 64
        N_MIX1 = S_OUT1 - S_MIX1

        def tiles_of(s):
            return HALF if any(a <= s < a + 2 * KD for a in S_DN) else KD

        def pieces_of(s):
            if S_QB <= s < S_QB + 4:
                return 2
            return 3 if S_MERGE <= s < S_OUT2 and s % 2 else 1

        landed_at, total = [], [0, 0]
        for s_ in range(N_SLABS):
            total[s_ % 2] += 16 * pieces_of(s_)
            landed_at.append(total[s_ % 2])

        rows_landed, x_landed, const_landed = sem("rows_landed"), sem("x_landed"), sem("const_landed")
        lam_landed, dist_landed, table_landed = sem("lam_landed"), sem("dist_landed"), sem("table_landed")
        rpb_copied = sem("rpb_copied")
        wpool_landed, count_landed, out_landed = sem("wpool_landed"), sem("count_landed"), sem("out_landed")
        raw_landed = [sem("raw_landed0"), sem("raw_landed1")]
        near_landed = [sem("near_landed0"), sem("near_landed1")]
        ada_landed = [sem(f"ada_landed{j}") for j in range(4)]
        row_landed = [sem("row_landed0"), sem("row_landed1")]
        mod_summed, scale_summed = sem("mod_summed"), sem("scale_summed")
        w_high, w_ready, w_used = sem("w_high"), sem("w_ready"), sem("w_used")
        filled = [sem(f"bank_filled{b}") for b in range(8)]
        emptied = [sem(f"bank_emptied{b}") for b in range(8)]
        consts_set, lam_set = sem("consts_set"), sem("lam_set")
        lam_exp, lam_prod = sem("lam_exp"), sem("lam_prod")
        cact_set, x_rms, xn_set, mod_set, x_root = sem("cact_set"), sem("x_rms"), sem("xn_set"), sem("mod_set"), sem("x_root")
        h_high, h_whole, h_ready = sem("h_high"), sem("h_whole"), sem("h_ready")
        v_high = sem("v_high")
        alibi_set, expd, combined, wt_high = sem("alibi_set"), sem("expd"), sem("combined"), sem("wt_high")
        pads_set, pooled, conved = sem("pads_set"), sem("pooled"), sem("conved")
        o_squared, sub_scaled, y_set = sem("o_squared"), sem("sub_scaled"), sem("y_set")
        squared, summed = sem("squared"), sem("summed")
        cols_set, scale_set, root2 = sem("cols_set"), sem("scale_set"), sem("root2")
        scaled_x = sem("scaled_x")
        gate_scaled, gate_act, hid_set, hid_high, hid_ready = (sem(n) for n in (
            "gate_scaled", "gate_act", "hid_set", "hid_high", "hid_ready"))
        x_new = sem("x_new")
        roped, y2_high = sem("roped"), sem("y2_high")
        expd2, combined2, wt2_high, near_set = sem("expd2"), sem("combined2"), sem("wt2_high"), sem("near_set")
        sa_set, sb_set, merged, m_high, m_ready = sem("sa_set"), sem("sb_set"), sem("merged"), sem("m_high"), sem("m_ready")
        o_final, tok_set = sem("o_final"), [sem("tok_set0"), sem("tok_set1")]
        scored2, branch_set, t_set = sem("scored2"), sem("branch_set"), sem("t_set")
        dve_step, pool_step = sem("dve_step"), sem("pool_step")

        SQUARES = {"out1": 0, "down0": 8, "down1": 24, "out2": 32, "down2": 40}
        NEW_X = {"out1": 0, "down0": 8, "down1": 16, "out2": 24, "down2": 32}
        SUM0 = 2
        GEN = {"proj1": 0, "y": 1, "ffn0": 2, "ffn1": 3, "mix2": 4, "ffn2": 5}

        bank, before, full, free_at = {}, {}, {}, {}
        last_turn, n_full, n_free = {}, [0] * 8, [0] * 8

        def plan(name, b, complete=None, read=None):
            if complete is None:
                n_full[b] += 1
                complete = (filled[b], n_full[b])
            if read is None:
                n_free[b] += 1
                read = (emptied[b], n_free[b])
            bank[name], before[name], full[name], free_at[name] = b, last_turn.get(b), complete, read
            last_turn[b] = name

        def plan_slab(name, b, s, read=None):
            plan(name, b, (w_used, s + 1), read)

        plan("vectors", 7)
        for k in range(KD):
            plan(("x", k), k % 4)
        plan(("shift", 0), 4)
        for k in range(KD):
            plan(("xn", k), 4 + k % 3)
        plan(("shift", 1), 5)
        plan(("mod", 0), 7)
        for i in range(TT):
            plan_slab(("v1", i), i, S_V + 3)
        plan(("mod", GT1 // KD), 4)
        plan_slab(("slab", S_Q0), 7, S_Q0)
        plan_slab(("slab", S_Q0 + 1), 6, S_Q0 + 1)
        for u in range(UN1):
            for m in range(2):
                plan(("s1", u, m), 2 * (u % 2) + m)
            plan(("t1", u), 4 + u % 2)
        for g in range(UN1 // 2):
            if 2 * g + 4 in MOD_STEP:
                plan(("mod", MOD_STEP[2 * g + 4]), 6)
            plan(("o1", g), 6)
        for s_ in range(S_MIX1, S_OUT1):
            plan_slab(("slab", s_), 7, s_)
        plan(("pool", 0), 0)
        plan(("pool", 1), 1)
        plan("sub_sum", 7)
        for c in range(4):
            plan(("sub", c), c, read=(y_set, c + 1))

        def plan_scale(name, nth, two=False):
            plan(("sum", name), 6)
            if name == "ffn0":
                plan(("scale", name), 7, read=(scaled_x, KD))
            elif two:
                plan(("scale", name), 7)
                plan(("scale2", name), 6, read=(scale_set, nth))
            else:
                plan(("scale", name), 7, read=(scale_set, nth))

        def plan_ffn(f):
            for n in range(KF):
                m, s = KF * f + n + 1, S_GU[f] + 2 * n
                plan_slab(("gate", f, n), 4 if n == 0 else 0, s, (gate_scaled, m - KF) if f else (gate_act, m))
                plan_slab(("up", f, n), 5 if n == 0 else 1, s + 1, (hid_set, m))
            if f == 0:
                plan(("mod", GT2 // KD), 7)
            for n in range(KD):
                plan_slab(("down", f, n), 2 + n % 2, S_DN[f] + 2 * n + 1,
                          (t_set, KD * (f - 1) + n + 1) if f else (x_new, NEW_X["down0"] + n + 1))

        for n in range(KD):
            plan_slab(("out1", n), 4 + n % 2, S_OUT1 + n, (x_new, NEW_X["out1"] + n + 1))
        plan_scale("ffn0", 0)
        plan_ffn(0)
        plan_scale("ffn1", 1, two=True)
        plan_ffn(1)
        for i in range(TT):
            plan_slab(("va", i), i, S_PROJ2 + 3)
        plan_scale("mix2", 2)
        plan_slab("vb", 4, S_PROJ2 + 4)
        plan_slab("kb", 5, S_PROJ2 + 5, (roped, 1))
        plan("kb_turn", 6)
        for c in range(4):
            plan_slab(("qb", c), 7 if c % 2 == 0 else 5, S_QB + c, (roped, 3 + 2 * c))
            plan(("qb_turn", c), 4 if c % 2 == 0 else 6)
        for u in range(UN2):
            plan(("s2", u), u % 3, read=None if u < UN2 // 2 else (scored2, u + 1))
            plan(("t2", u), 4 + u % 2)
        for g in range(UN2 // 2):
            plan(("o2", g), 6)
        for s_ in range(S_MIX2, S_MERGE):
            plan_slab(("slab", s_), 3 if s_ % 2 else 7, s_)
        for n in range(KD):
            plan_slab(("gb", n), 0, S_MERGE + 2 * n, (sb_set, n + 1))
            plan(("a", n), 1, read=(branch_set, 2 * n + 1))
            plan_slab(("b", n), 2, S_MERGE + 2 * n + 1, (branch_set, 2 * n + 2))
        for n in range(KD):
            plan_slab(("out2", n), 4 + n % 2, S_OUT2 + n, (x_new, NEW_X["out2"] + n + 1))
        plan_scale("ffn2", 3)
        plan_ffn(2)
        for i in range(TT):
            if i == TT - 1:
                plan(("sum", "last"), 6)
            for half in range(2):
                plan(("fin", i, half), 2 * i + half)

        def along(value, n, i=None, step=1):
            v = value(n)
            return v if i is None else i * (value(n + step) - v) + v

        def slot_of(n, i=None, step=1):
            return bass.ds(n if i is None else i * step + n, 1)

        N_CONSTS = 7
        YS = [6, 7, 4, 5, 0, 1, 2, 3]
        KINDS1 = [("q", 1), ("k", 1), ("cg", 0), ("u", 0), ("u", 1), ("q", 2), ("k", 2), ("cg", 1),
                  ("q", 3), ("k", 3), ("xc", 0), ("xc", 1), ("bg", 0), ("bg", 1)]

        def unit2(u):
            windowed, v = u < UN2 // 2, u % (UN2 // 2)
            c, j, i = v // 8, v % 8 // 4, v % 4
            if windowed:
                return True, c, j, i, c + 4 * j, list(range(max(0, i - 1), min(TT, i + 2)))
            return False, c, j, i, 2 * c + j, list(range(TT))

        def exps2(u):
            return 2 * (u + 1) if u < UN2 // 2 else UN2 + u + 1 - UN2 // 2

        def wait_filled(eng, name, n=None, i=None, step=1):
            key = name if n is None else (*name, n)
            s_, v = full[key]
            if i is not None:
                v = along(lambda m: full[(*name, m)][1], n, i, step)
            eng.wait_ge(s_, v)
            return bank[key]

        def wait_emptied(eng, name):
            eng.wait_ge(*free_at[name])

        block = ctx.enter_context(nc.Block())

        @block.tensor
        def _(pe):
            def bank_of(name):
                return bank[name]

            def take(name, n=None, i=None, step=1):
                key = name if n is None else (*name, n)
                if i is not None:
                    key = (*name, n)
                    assert before[key] == (*name, n - step)
                    pe.wait_ge(free_at[key][0], along(lambda m: free_at[(*name, m)][1], n - step, i, step))
                elif before[key] is not None:
                    pe.wait_ge(*free_at[before[key]])
                return bank[key]

            def three(o, a_hi, a_lo, b_hi, b_lo, start, stop):
                pe.matmul(o, a_hi, b_hi, start=start, stop=False)
                pe.matmul(o, a_hi, b_lo, start=False, stop=False)
                return pe.matmul(o, a_lo, b_hi, start=False, stop=stop)

            def tile(s, j):
                return w_hi[:, s % 2, P * j:P * j + P], w_lo[:, s % 2, P * j:P * j + P]

            def await_slab(s, i=None, step=1):
                pe.wait_ge(w_ready, s + 1 if i is None else i * step + s + 1)

            def chunk(o, s, js, xs, ready=None, start=True, stop=True):
                last = None
                for n, (j, (b_hi, b_lo)) in enumerate(zip(js, xs)):
                    if ready is not None:
                        pe.wait_ge(ready[0], ready[1] + n + 1)
                    w = tile(s, j)
                    last = three(o, *w, b_hi, b_lo, start and n == 0, stop and n == len(js) - 1)
                return last

            hs = [(h_hi[:, k, :], h_lo[:, k, :]) for k in range(KD)]

            pe.wait_ge(const_landed, 32)
            pe.wait_ge(rows_landed, 16 * len(VECTORS))
            pe.transpose(psum[:, 7, 0:N_ROWS], rows[0:N_ROWS, :], ident[0:N_ROWS, 0:N_ROWS]).then_inc(filled[7], 1)
            pe.wait_ge(x_landed, 16 * TT)
            def turned(src, name):
                for k in range(KD):
                    b = take((name, k))
                    for i in range(TT):
                        last = pe.transpose(psum[:, b, P * i:P * i + P], src[:, i, P * k:P * k + P], ident[:, :])
                    last.then_inc(filled[b], 1)

            def shift_rows(j):
                pe.wait_ge(ada_landed[j], 16)
                b = take(("shift", j))
                for k in range(KD):
                    last = pe.matmul(psum[0:1, b, :], cact[:, k:k + 1], ada_w[:, j, T * k:T * k + T],
                                     start=k == 0, stop=k == KD - 1)
                last.then_inc(filled[b], 1)

            turned(x_tok, "x")
            pe.wait_ge(cact_set, 1)
            shift_rows(0)
            pe.wait_ge(xn_set, TT)
            turned(xn_tok, "xn")
            shift_rows(1)
            pe.wait_ge(consts_set, N_CONSTS)
            b = take(("mod", 0))
            for j in range(2):
                wait_emptied(pe, ("shift", j))
            for n in range(KD):
                pe.matmul(psum[:, b, n:n + 1], mod_row[0:1, P * n:P * n + P], one_col[0:1, :], start=True, stop=True)
            pe.wait_ge(scale_summed, 2)
            for n in range(KD):
                last = pe.matmul(psum[:, b, KD + n:KD + n + 1], first_acc[:, P * n:P * n + P], one_col,
                                 start=True, stop=True)
            last.then_inc(filled[b], 1)

            def mod_columns(j):
                pe.wait_ge(consts_set, N_CONSTS)
                pe.wait_ge(mod_summed, j - 1)
                b = take(("mod", j))
                for n in range(KD):
                    last = pe.matmul(psum[:, b, n:n + 1], mod_acc[:, P * n:P * n + P], one_col, start=True, stop=True)
                last.then_inc(filled[b], 1)

            for s in range(S_V, S_V + 4):
                await_slab(s)
                for i in range(TT):
                    b = take(("v1", i)) if s == S_V else i
                    for j in range(2):
                        k = 2 * (s - S_V) + j
                        pe.wait_ge(h_ready, k + 1)
                        ts = slice(P * i, P * i + P)
                        ws = slice(T * j, T * j + T)
                        last = three(psum[:, b, :], h_hi[:, k, ts], h_lo[:, k, ts], w_hi[:, s % 2, ws],
                                     w_lo[:, s % 2, ws], k == 0, k == KD - 1)
                last.then_inc(w_used, 1)

            def whole(name, s, xs=hs, ready=None):
                await_slab(s)
                b = take(name)
                last = chunk(psum[:, b, :], s, range(KD), xs, ready)
                last.then_inc(w_used, 1)

            whole(("slab", S_Q0), S_Q0)
            mod_columns(GT1 // KD)
            whole(("slab", S_Q0 + 1), S_Q0 + 1)

            def part(s, q, parts):
                n = KD // parts
                if q == 0:
                    await_slab(s)
                    take(("slab", s))
                b = bank_of(("slab", s))
                last = chunk(psum[:, b, :], s, range(n * q, n * q + n), hs[n * q:n * q + n], None, q == 0, q == parts - 1)
                if q == parts - 1:
                    last.then_inc(w_used, 1)

            for t in range(UN1 + 4):
                if t < UN1:
                    h, i = t // 4, t % 4
                    c = h // 2
                    if t % 8 == 0:
                        for n, kind in enumerate("qk"):
                            wait_emptied(pe, ("slab", S_MIX1 + KINDS1.index((kind, c)) if c else S_Q0 + n))
                    for m in range(2):
                        b = take(("s1", t, m))
                        r = DH * (h % 2) + DQ1 * m
                        pe.matmul(psum[:, b, :], q1[r:r + DQ1, c, P * i:P * i + P], k1[r:r + DQ1, c, :],
                                  start=True, stop=True).then_inc(filled[b], 1)
                if t < 2 * N_MIX1:
                    part(S_MIX1 + t // 2, t % 2, 2)
                u = t - 2
                if 0 <= u < UN1:
                    pe.wait_ge(combined, u + 1)
                    b = take(("t1", u))
                    for kt in range(TT):
                        last = pe.transpose(psum[:, b, P * kt:P * kt + P], p1[:, u % 3, 0, P * kt:P * kt + P], ident[:, :])
                    last.then_inc(filled[b], 1)
                if t >= 5 and t % 2:
                    g = (t - 5) // 2
                    c = g // 4
                    if g == 0:
                        for kt in range(TT):
                            wait_emptied(pe, ("v1", kt))
                    wait_emptied(pe, ("t1", 2 * g))
                    wait_emptied(pe, ("t1", 2 * g + 1))
                    b = take(("o1", g))
                    for kt in range(TT):
                        last = three(psum[:, b, 0:2 * P], v1_hi[:, kt, P * c:P * c + P], v1_lo[:, kt, P * c:P * c + P],
                                     wt_hi[:, g % 2, kt, :], wt_lo[:, g % 2, kt, :], kt == 0, kt == TT - 1)
                    last.then_inc(filled[b], 1)
                if t in MOD_STEP:
                    mod_columns(MOD_STEP[t])
                if t == UN1:
                    pe.wait_ge(wpool_landed, 64)
                    pe.wait_ge(pooled, 2)
                    for c2, src in enumerate((pool_d, pool_t)):
                        b = take(("pool", c2))
                        pe.matmul(psum[:, b, :], wpool_bd[:, c2, :], src[:, :], start=True, stop=True)\
                          .then_inc(filled[b], 1)

            for n in range(2):
                await_slab(S_OUT1 + n)
                b = take(("out1", n))
                chunk(psum[:, b, :], S_OUT1 + n, YS[0:4], [hs[k] for k in YS[0:4]], (h_ready, 8 * GEN["y"]), stop=False)

            b = take("sub_sum")
            pe.wait_ge(consts_set, N_CONSTS)
            for c in range(4):
                pe.wait_ge(o_squared, c + 1)
                for i in range(TT):
                    last = pe.matmul(psum[:, b, 8 * i + 2 * c:8 * i + 2 * c + 2], q1[:, c, P * i:P * i + P], mean_h,
                                     start=True, stop=True)
            last.then_inc(filled[b], 1)
            pe.wait_ge(sub_scaled, 1)
            for c in range(4):
                b = take(("sub", c))
                for i in range(TT):
                    for j in range(2):
                        at = 8 * i + 2 * c + j
                        last = pe.matmul(psum[DH * j:DH * j + DH, b, P * i:P * i + P],
                                         rsub[:, at:at + 1].to_broadcast([P, DH]), ident[:, :], start=True, stop=True)
                last.then_inc(filled[b], 1)

            def out_proj(key, s0, xs, js, ready):
                def two(n0, i=None):
                    for n in (n0, n0 + 1):
                        await_slab(s0 + n, i, 2)
                        b = take((key,), n, i, 2)
                        chunk(psum[:, b, :], s0 + n, js, xs, ready).then_inc(w_used, 1)

                if key == "out1":
                    for n in range(2):
                        chunk(psum[:, bank_of((key, n)), :], s0 + n, js[4:], xs[4:], (ready[0], ready[1] + 4),
                              start=False).then_inc(w_used, 1)
                else:
                    two(0)
                with repeat(pe, KD // 2 - 1, []) as i:
                    two(2, i)

            out_proj("out1", S_OUT1, [hs[k] for k in YS], YS, (h_ready, 8 * GEN["y"]))

            def token_sums(name, phase, kinds=1):
                pe.wait_ge(summed, SUM0 + SQUARES[phase] + KD * kinds)
                b = take(("sum", name))
                for m in range(kinds):
                    for i in range(TT):
                        last = pe.matmul(psum[:, b, 4 * m + i:4 * m + i + 1], acc[:, m, P * i:P * i + P], mean_d,
                                         start=True, stop=True)
                last.then_inc(filled[b], 1)

            def spread(key, col, ready):
                pe.wait_ge(cols_set, ready)
                b = take(key)
                for i in range(TT):
                    last = pe.matmul(psum[:, b, P * i:P * i + P], rcol[:, col + i:col + i + 1].to_broadcast([P, P]),
                                     ident[:, :], start=True, stop=True)
                last.then_inc(filled[b], 1)

            token_sums("ffn0", "out1")
            spread(("scale", "ffn0"), 4, 1)

            def ffn(f, between):
                s0 = S_GU[f]
                h0 = 8 * GEN[f"ffn{f}"]

                def pair(n, i=None):
                    for key, sl in (("gate", 0), ("up", 1)):
                        await_slab(s0 + 2 * n + sl, i, 2)
                        b = take((key, f), n, i)
                        chunk(psum[:, b, :], s0 + sl, range(KD), hs, (h_ready, h0)).then_inc(w_used, 1)
                        if n == 0 and sl == 0:
                            between()

                def down_pair(n0, i=None):
                    for n in (n0, n0 + 1):
                        for half in range(2):
                            s = S_DN[f] + 2 * n + half
                            await_slab(s, i, 4)
                            b = take(("down", f), n, i, 2) if half == 0 else bank_of(("down", f, n))
                            ks = range(HALF * half, HALF * half + HALF)
                            chunk(psum[:, b, :], s, range(HALF), [(hid_hi[:, k, :], hid_lo[:, k, :]) for k in ks],
                                  (hid_ready, KF * f + HALF * half), half == 0, half == 1).then_inc(w_used, 1)

                pair(0)
                pair(1)
                with repeat(pe, KF - 2, []) as i:
                    pair(2, i)
                if f == 0:
                    mod_columns(GT2 // KD)
                down_pair(0)
                with repeat(pe, KD // 2 - 1, []) as i:
                    down_pair(2, i)

            ffn(0, lambda: None)

            def scale_ffn1():
                token_sums("ffn1", "down0", 2)
                spread(("scale", "ffn1"), 8, 2)
                spread(("scale2", "ffn1"), 4, 3)

            ffn(1, scale_ffn1)

            for s in range(S_PROJ2, S_PROJ2 + 4):
                await_slab(s)
                for i in range(TT):
                    b = take(("va", i)) if s == S_PROJ2 else i
                    for j in range(2):
                        k = 2 * (s - S_PROJ2) + j
                        pe.wait_ge(h_ready, 8 * GEN["mix2"] + k + 1)
                        ts = slice(P * i, P * i + P)
                        ws = slice(T * j, T * j + T)
                        last = three(psum[:, b, :], h_hi[:, k, ts], h_lo[:, k, ts], w_hi[:, s % 2, ws],
                                     w_lo[:, s % 2, ws], k == 0, k == KD - 1)
                last.then_inc(w_used, 1)
                if s == S_PROJ2:
                    token_sums("mix2", "down1")
                    spread(("scale", "mix2"), 4, 4)
            s = S_PROJ2 + 4
            await_slab(s)
            b = take("vb")
            for i in range(TT):
                for k in range(KD):
                    w = tile(s, k)
                    last = three(psum[:, b, P * i:P * i + P], h_hi[:, k, P * i:P * i + P], h_lo[:, k, P * i:P * i + P],
                                 *w, k == 0, k == KD - 1)
            last.then_inc(w_used, 1)

            def rope_turn(name, src, n):
                pe.wait_ge(roped, n)
                b = take(name)
                pe.matmul(psum[:, b, :], turn_m[:, :], src, start=True, stop=True).then_inc(filled[b], 1)

            whole("kb", S_PROJ2 + 5)
            for c in range(4):
                whole(("qb", c), S_QB + c)
                if c == 0:
                    rope_turn("kb_turn", kb[:, :], 1)
                else:
                    rope_turn(("qb_turn", c - 1), qb[:, c - 1, :], 1 + 2 * c)

            for t in range(UN2 + 4):
                if t == 1:
                    rope_turn(("qb_turn", 3), qb[:, 3, :], 9)
                if t < UN2:
                    windowed, c, j, i, head, kts = unit2(t)
                    r = DH * j
                    if windowed and t % 8 == 0:
                        pe.wait_ge(roped, 4 + 2 * c)
                    if not windowed and t % 8 == 0:
                        wait_emptied(pe, ("slab", S_MIX2 + 2 * c))
                        wait_emptied(pe, ("slab", S_MIX2 + 2 * c + 1))
                    b = take(("s2", t))
                    ks = slice(P * kts[0], P * kts[-1] + P)
                    if windowed:
                        q_, k_ = qb[r:r + DH, c, P * i:P * i + P], kb[r:r + DH, ks]
                    else:
                        q_, k_ = qa[r:r + DH, c, P * i:P * i + P], ka[r:r + DH, c, ks]
                    pe.matmul(psum[:, b, 0:P * len(kts)], q_, k_, start=True, stop=True).then_inc(filled[b], 1)
                    part(S_MIX2 + t // 4, t % 4, 4)
                u = t - 2
                if 0 <= u < UN2:
                    kts = unit2(u)[5]
                    pe.wait_ge(combined2, u + 1)
                    b = take(("t2", u))
                    for n in range(len(kts)):
                        last = pe.transpose(psum[:, b, P * n:P * n + P], p2[:, u % 3, P * n:P * n + P], ident[:, :])
                    last.then_inc(filled[b], 1)
                if t >= 5 and t % 2:
                    g = (t - 5) // 2
                    windowed, c = unit2(2 * g)[0:2]
                    if g == 0:
                        wait_emptied(pe, "vb")
                        for kt in range(TT):
                            wait_emptied(pe, ("va", kt))
                    wait_emptied(pe, ("t2", 2 * g))
                    wait_emptied(pe, ("t2", 2 * g + 1))
                    b = take(("o2", g))
                    if not windowed:
                        sees = [(kt, 0, 2 * P) for kt in range(TT)]
                    elif g % 2 == 0:
                        sees = [(0, 0, 2 * P), (1, 0, 2 * P), (2, P, 2 * P)]
                    else:
                        sees = [(2, 0, 2 * P), (3, 0, 2 * P), (1, 0, P)]
                    for n, (kt, c0, c1) in enumerate(sees):
                        if windowed:
                            v_ = vb_hi[:, kt, :], vb_lo[:, kt, :]
                        else:
                            v_ = va_hi[:, kt, P * c:P * c + P], va_lo[:, kt, P * c:P * c + P]
                        last = three(psum[:, b, c0:c1], *v_, wt2_hi[:, g % 2, kt, c0:c1], wt2_lo[:, g % 2, kt, c0:c1],
                                     n == 0, n == len(sees) - 1)
                    last.then_inc(filled[b], 1)

            wait_emptied(pe, ("o2", UN2 // 2 - 1))
            ab = [(ya_hi[:, k, :], ya_lo[:, k, :]) for k in range(4)], [(yb_hi[:, k, :], yb_lo[:, k, :]) for k in range(4)]

            def gates(n, i=None):
                await_slab(S_MERGE + 2 * n, i, 2)
                b = take(("gb",), n, i)
                chunk(psum[:, b, :], S_MERGE, range(KD), hs).then_inc(w_used, 1)
                await_slab(S_MERGE + 2 * n + 1, i, 2)
                b = take(("a",), n, i)
                chunk(psum[:, b, :], S_MERGE + 1, range(0, 4), ab[0]).then_inc(filled[b], 1)
                b = take(("b",), n, i)
                chunk(psum[:, b, :], S_MERGE + 1, range(4, 8), ab[1]).then_inc(w_used, 1)

            gates(0)
            with repeat(pe, KD - 1, []) as i:
                gates(1, i)

            out_proj("out2", S_OUT2, [(m_hi[:, k, :], m_lo[:, k, :]) for k in range(KD)], range(KD), (m_ready, 0))

            def scale_ffn2():
                token_sums("ffn2", "out2")
                spread(("scale", "ffn2"), 4, 5)

            ffn(2, scale_ffn2)

            for i in range(TT):
                if i == TT - 1:
                    token_sums("last", "down2")
                for half in range(2):
                    b = take(("fin", i, half))
                    for k in range(4):
                        kk = 4 * half + k
                        pe.wait_ge(o_final, kk + 1)
                        last = pe.transpose(psum[:, b, P * k:P * k + P], o_scaled[:, kk, P * i:P * i + P], ident[:, :])
                    last.then_inc(filled[b], 1)

        @block.sync
        def _(sp):
            for i in range(TT):
                sp.dma_start(x_tok[:, i, :], ins["x"][0, P * i:P * i + P, :]).then_inc(x_landed, 16)
            ada = ins["w_ada"][0].rearrange("(k p) n -> p k n", p=P)
            sp.wait_ge(rows_landed, 16 * len(VECTORS))
            for j in (0, 2, 1, 3):
                sp.dma_start(ada_w[:, j, :].rearrange("p (k n) -> p k n", k=KD), ada[:, :, T * j:T * j + T])\
                  .then_inc(ada_landed[j], 16)

            def free(s, i=None, step=1):
                if s >= 2:
                    sp.wait_ge(w_ready, s - 1 if i is None else i * step + s - 1)

            def raw(s, j0=0, j1=KD, n=P):
                return w_raw[:, s % 2, j0 * P:j1 * P].rearrange("p (k n) -> p k n", n=n)

            def load(s, src, j0=0, j1=KD, n=P):
                sp.dma_start(raw(s, j0, j1, n), src).then_inc(raw_landed[s % 2], 16)

            w1 = ins["w_in"][0].rearrange("(k p) n -> p k n", p=P)
            AW, PW = 4 * P, 2 * P
            o_k, o_v, o_p, o_b, o_c, o_x = AW, 2 * AW, 3 * AW, 3 * AW + PW, 3 * AW + 2 * PW, 3 * AW + 3 * PW
            first = {"q": 0, "k": o_k, "u": o_p, "cg": o_c, "xc": o_x, "bg": o_b}
            for s in range(4):
                free(s)
                load(s, w1[:, 2 * s:2 * s + 2, o_v:o_v + T], n=T)
            for n, (kind, c) in enumerate([("q", 0), ("k", 0), *KINDS1]):
                free(S_Q0 + n)
                load(S_Q0 + n, w1[:, :, first[kind] + P * c:first[kind] + P * c + P])

            def columns(s0, w):
                src = w.rearrange("(k p) n -> p k n", p=P)
                with repeat(sp, KD // 2, []) as i:
                    for n in range(2):
                        free(s0 + n, i, 2)
                        load(s0 + n, src[:, :, bass.ds(i * 2 * P + P * n, P)])

            def ffn(f, w_gate, w_up, w_down):
                gate, up = (w.rearrange("(k p) n -> p k n", p=P) for w in (w_gate, w_up))
                with repeat(sp, KF, []) as i:
                    for n, src in enumerate((gate, up)):
                        free(S_GU[f] + n, i, 2)
                        load(S_GU[f] + n, src[:, :, bass.ds(i * P, P)])
                down = w_down.rearrange("(k p) n -> p k n", p=P)
                with repeat(sp, KD, []) as i:
                    for n in range(2):
                        free(S_DN[f] + n, i, 2)
                        load(S_DN[f] + n, down[:, HALF * n:HALF * n + HALF, bass.ds(i * P, P)], 0, HALF)

            columns(S_OUT1, ins["w_out"][0])
            wgu = ins["w_gate_up"][0]
            ffn(0, wgu[:, 0:FF], wgu[:, FF:2 * FF], ins["w_down"][0])
            ffn(1, ins["ffn1_w_gate_2"][0], ins["ffn1_w_up_2"][0], ins["ffn1_w_down_2"][0])

            w2 = ins["w_in_2"][0].rearrange("(k p) n -> p k n", p=P)
            o_qb, o_kb, o_vb, o_ga, o_gb = 3 * AW, 4 * AW, 4 * AW + P, 4 * AW + 2 * P, 4 * AW + 2 * P + D
            for s in range(4):
                free(S_PROJ2 + s)
                load(S_PROJ2 + s, w2[:, 2 * s:2 * s + 2, o_v:o_v + T], n=T)
            for n, at in enumerate((o_vb, o_kb)):
                free(S_PROJ2 + 4 + n)
                load(S_PROJ2 + 4 + n, w2[:, :, at:at + P])
            for c in range(4):
                free(S_QB + c)
                for j in range(2):
                    at = o_qb + DH * (c + 4 * j)
                    sp.dma_start(raw(S_QB + c)[:, :, DH * j:DH * j + DH], w2[:, :, at:at + DH])\
                      .then_inc(raw_landed[(S_QB + c) % 2], 16)
            for j in range(16):
                at = [P * (j // 2), o_k + P * (j // 2)][j % 2] if j < 8 else o_ga + P * (j - 8)
                free(S_MIX2 + j)
                load(S_MIX2 + j, w2[:, :, at:at + P])
            wa = ins["w_branch_a_2"][0].rearrange("(k p) n -> p k n", p=P)
            wb = ins["w_branch_b_2"][0].rearrange("(j k p) n -> p j k n", p=DH, k=4)
            for n in range(KD):
                s, cols = S_MERGE + 2 * n, slice(P * n, P * n + P)
                free(s)
                load(s, w2[:, :, o_gb + P * n:o_gb + P * n + P])
                free(s + 1)
                load(s + 1, wa[:, :, cols], 0, 4)
                for j in range(2):
                    sp.dma_start(raw(s + 1, 4, 8)[DH * j:DH * j + DH], wb[:, j, :, cols])\
                      .then_inc(raw_landed[1], 16)
            columns(S_OUT2, ins["w_out_2"][0])
            ffn(2, ins["ffn2_w_gate_2"][0], ins["ffn2_w_up_2"][0], ins["ffn2_w_down_2"][0])
            for i in range(TT):
                for side in tok_set:
                    sp.wait_ge(side, i + 1)
                sp.dma_start(out[0, P * i:P * i + P, :], o_tok[:, i, :]).then_inc(out_landed, 16)
            sp.wait_ge(out_landed, 16 * TT)

        @block.scalar
        def _(act):
            for name, n in VECTORS:
                r = ROW_OF[name]
                act.dma_start(rows[r:r + n, :], ins[name]).then_inc(rows_landed, 16)
            act.dma_start(ident[:, :], ins["k_ident"]).then_inc(const_landed, 16)
            act.dma_start(turn_m[:, :], ins["k_turn"]).then_inc(const_landed, 16)
            for n, name in enumerate(("lambda_q1", "lambda_q2", "lambda_k1", "lambda_k2")):
                act.dma_start(lamrow[:, DQ1 * n:DQ1 * n + DQ1], ins[name].to_broadcast([P, DQ1]))\
                   .then_inc(lam_landed, 16)
            act.dma_start(sink, ins["sink_logit_2"].to_broadcast([P, H])).then_inc(lam_landed, 16)
            for c in range(2):
                act.dma_start(count_sb[c], ins["k_count"][:, c, :]).then_inc(count_landed, 16)

            def split_high(s, i=None, step=1):
                act.wait_ge(raw_landed[s % 2], along(lambda m: landed_at[m], s, i, step))
                if s >= 2:
                    act.wait_ge(w_used, s - 1 if i is None else i * step + s - 1)
                n = tiles_of(s) * P
                act.activation(w_hi[:, s % 2, 0:n], w_raw[:, s % 2, 0:n], ACT.Identity).then_inc(w_high, 1)

            wait_emptied(act, "vectors")
            c0 = ROW_OF["c"]
            act.activation(cact[:, :], vcol[:, c0:c0 + KD], ACT.Silu).then_inc(cact_set, 1)
            act.wait_ge(x_landed, 16 * TT)
            for i in range(TT):
                if i:
                    act.wait_ge(x_rms, i)
                act.activation(junk[:, :], x_tok[:, i, :], ACT.Square, accum_out=rcol[:, i:i + 1]).then_inc(x_rms, 1)
            act.wait_ge(x_rms, TT)
            act.wait_ge(consts_set, N_CONSTS)
            act.activation(rcol[:, 4:8], rcol[:, 0:4], ACT.Sqrt, bias=eps, scale=1.0 / D).then_inc(x_root, 1)
            def keep_shift(j):
                b = wait_filled(act, ("shift", j))
                act.activation(mod_row[0:1, T * j:T * j + T], psum[0:1, b, :], ACT.Identity).then_inc(emptied[b], 1)

            keep_shift(0)
            for k in range(KD):
                b = wait_filled(act, ("xn", k))
                act.activation(xn_t[:, k, :], psum[:, b, :], ACT.Identity).then_inc(emptied[b], 1)
            act.wait_ge(lam_prod, 1)
            act.activation(lamrow[:, 194:196], lamrow[:, 192:194], ACT.Exp).then_inc(lam_exp, 1)
            keep_shift(1)
            act.wait_ge(mod_set, 1)
            act.dma_start(dist[:, :], ins["k_dist"]).then_inc(dist_landed, 16)
            for k in range(KD):
                wait_emptied(act, ("xn", k))
                act.activation(h_hi[:, k, :], xn_t[:, k, :], ACT.Identity, bias=modc[:, SH1 + k:SH1 + k + 1],
                               scale=scale1[:, k:k + 1]).then_inc(h_high, 1)
                if k in (0, 2):
                    split_high(k // 2)

            def alibi_table(h):
                if h >= 2:
                    for m in range(2):
                        wait_emptied(act, ("s1", 4 * (h - 2) + 3, m))
                else:
                    act.wait_ge(dist_landed, 16)
                act.activation(alibi[:, h % 2, :], dist[:, :], ACT.Copy, scale=2.0 ** (-8.0 * (h + 1) / H))\
                   .then_inc(alibi_set, 1)

            alibi_table(0)
            for s in range(2, 5):
                split_high(s)
            for i in range(TT):
                b = wait_filled(act, ("v1", i))
                act.activation(v1_hi[:, i, :], psum[:, b, :], ACT.Identity).then_inc(v_high, 1)

            def keep_q1(name, c):
                b = wait_filled(act, name)
                act.activation(q1[:, c, :], psum[:, b, :], ACT.Copy, scale=-float(DQ1) ** -0.5).then_inc(emptied[b], 1)

            def keep_k1(name, c):
                b = wait_filled(act, name)
                act.activation(k1[:, c, :], psum[:, b, :], ACT.Copy).then_inc(emptied[b], 1)

            split_high(5)
            keep_q1(("slab", S_Q0), 0)
            split_high(6)
            keep_k1(("slab", S_Q0 + 1), 0)

            for t in range(UN1 + 5):
                if t == UN1 + 3:
                    for c in range(2):
                        b = wait_filled(act, ("pool", c))
                        p0 = ROW_OF["pool_scale"] + c
                        act.activation(y_side[:, c, :], psum[:, b, :], ACT.Copy, scale=vcol[:, p0:p0 + 1])\
                           .then_inc(emptied[b], 1)
                    for c in range(2):
                        wait_emptied(act, ("pool", c))
                        act.activation(h_hi[:, 4 + c, :], y_side[:, c, :], ACT.Identity).then_inc(h_high, 1)
                if t < 2 * N_MIX1 and t % 2 == 0:
                    split_high(S_MIX1 + t // 2 + 1)
                if 2 <= t <= 2 * N_MIX1 and t % 2 == 0:
                    j = t // 2 - 1
                    kind, c = KINDS1[j]
                    name = ("slab", S_MIX1 + j)
                    if kind == "q":
                        keep_q1(name, c)
                    elif kind == "k":
                        keep_k1(name, c)
                    elif kind == "u":
                        if c == 0:
                            act.wait_ge(pads_set, 1)
                        else:
                            act.wait_ge(pooled, 1)
                        b = wait_filled(act, name)
                        act.activation(pool_u[:, 8:8 + T], psum[:, b, :], ACT.Copy).then_inc(emptied[b], 1)
                    elif kind == "cg":
                        b = wait_filled(act, name)
                        act.activation(conv_c[:, c, :], psum[:, b, :], ACT.Copy).then_inc(emptied[b], 1)
                u = t - 3
                if 0 <= u < UN1:
                    g = u // 2
                    if g >= 2:
                        wait_filled(act, ("o1", g - 2))
                    b = wait_filled(act, ("t1", u))
                    act.activation(wt_hi[:, g % 2, :, P * (u % 2):P * (u % 2) + P],
                                   psum[:, b, :].rearrange("p (k q) -> p k q", k=TT), ACT.Copy).then_inc(wt_high, 1)
                if t >= 6 and t % 2 == 0:
                    g = (t - 6) // 2
                    h, a = g // 2, g % 2
                    r = DH * (h % 2)
                    b = wait_filled(act, ("o1", g))
                    act.activation(o1[r:r + DH, h // 2, 2 * P * a:2 * P * a + 2 * P], psum[r:r + DH, b, 0:2 * P], ACT.Copy)\
                       .then_inc(emptied[b], 1)
                if t < UN1:
                    if t % 4 == 0 and t // 4 + 1 < H:
                        alibi_table(t // 4 + 1)
                    for m in range(2):
                        wait_emptied(act, ("s1", t, m))
                        act.activation(p1[:, t % 3, m, :], p1[:, t % 3, m, :], ACT.Exp, bias=stat[:, t % 3, m:m + 1],
                                       scale=-1.0, accum_out=stat[:, t % 3, 2 + m:3 + m]).then_inc(expd, 1)
                if t == UN1:
                    act.wait_ge(w_used, S_OUT1)
                    for c in range(2):
                        wait_emptied(act, ("slab", S_MIX1 + KINDS1.index(("bg", c))))
                    for c in (2, 3):
                        act.activation(h_hi[:, 4 + c, :], y_side[:, c, :], ACT.Identity).then_inc(h_high, 1)
            split_high(S_OUT1 + 1)
            wait_emptied(act, ("o1", UN1 // 2 - 1))
            for c in range(4):
                act.activation(q1[:, c, :], o1[:, c, :], ACT.Square).then_inc(o_squared, 1)
            b = wait_filled(act, "sub_sum")
            act.activation(rsub[:, :], psum[:, b, 0:32], ACT.Sqrt, bias=eps).then_inc(emptied[b], 1)
            for c in range(4):
                act.wait_ge(y_set, c + 1)
                act.activation(h_hi[:, c, :], k1[:, c, :], ACT.Identity).then_inc(h_high, 1)

            def wait_summed(phase, n, i, kinds=1):
                v = SUM0 + SQUARES[phase] + kinds * (n - 1)
                act.wait_ge(summed, v if i is None else i * 2 * kinds + v)

            def square(n, i, m=0, scale=1.0):
                act.activation(sq[:, n % 2, m, :], x[:, slot_of(n, i, 2), :], ACT.Square, scale=scale).then_inc(squared, 1)

            def col_of(name, n, i, step):
                return vcol[:, slot_of(ROW_OF[name] + n, i, step)]

            def wait_new(phase, n, i, step):
                v = NEW_X[phase] + n + 1
                act.wait_ge(x_new, v if i is None else i * step + v)

            def next_h(n, i, step, col):
                act.activation(h_hi[:, slot_of(n, i, step), :], x[:, slot_of(n, i, step), :], ACT.Identity, scale=col)\
                   .then_inc(h_high, 1)

            def out_chunks(phase, s0, col=None):
                def pair(n0, i=None, split_already=None):
                    for n in (n0, n0 + 1):
                        wait_summed(phase, n, i)
                        if n != split_already:
                            split_high(s0 + n + 1, i, 2)
                        wait_new(phase, n, i, 2)
                        if col is not None:
                            next_h(n, i, 2, col_of(col, n, i, 2))
                        square(n, i)

                pair(0, None, 0 if phase == "out1" else None)
                with repeat(act, KD // 2 - 1, []) as i:
                    pair(2, i)

            out_chunks("out1", S_OUT1)

            def root(name):
                b = wait_filled(act, ("sum", name))
                act.activation(rcol[:, 0:4], psum[:, b, 0:4], ACT.Sqrt, bias=eps).then_inc(emptied[b], 1)

            root("ffn0")
            act.wait_ge(mod_set, 2)
            for k in range(KD):
                act.wait_ge(scaled_x, k + 1)
                if k >= 2:
                    act.wait_ge(h_ready, 8 * GEN["ffn0"] + k - 1)
                for dst, done_ in ((h_full[:, k % 2, :], h_whole), (h_hi[:, k, :], h_high)):
                    act.activation(dst, x_scaled[:, k % 2, :], ACT.Identity, bias=modc[:, SH2 + k:SH2 + k + 1],
                                   scale=scale2[:, k:k + 1]).then_inc(done_, 1)

            def ffn(f, between, down, last=False):
                s0 = S_GU[f]

                def pair(n, i=None):
                    split_high(s0 + 2 * n + 1, i, 2)
                    if n == 0:
                        between()
                    if f == 0:
                        b = wait_filled(act, ("gate", f), n, i)
                        act.activation(t_silu[:, :], psum[:, b, :], ACT.Silu).then_inc(gate_act, 1)
                    else:
                        v = KF * (f - 1) + n + 1
                        act.wait_ge(gate_scaled, v if i is None else i + v)
                        act.activation(t_silu[:, :], t_gate[:, :], ACT.Silu).then_inc(gate_act, 1)
                    split_high(s0 + 2 * n + 2, i, 2)
                    v = KF * f + n + 1
                    act.wait_ge(hid_set, v if i is None else i + v)
                    act.activation(hid_hi[:, slot_of(n, i), :], t_hid[:, :], ACT.Identity).then_inc(hid_high, 1)

                pair(0)
                with repeat(act, KF - 2, []) as i:
                    pair(1, i)
                pair(KF - 1)

                def down_pair(n0, i=None):
                    for n in (n0, n0 + 1):
                        s = S_DN[f] + 2 * n
                        wait_summed(f"down{f}", n, i, 2 if f == 0 else 1)
                        split_high(s + 1, i, 4)
                        if not (last and n == KD - 1):
                            split_high(s + 2, i, 4)
                        down(n, i)

                with repeat(act, KD // 2 - 1, []) as i:
                    down_pair(0, i)
                down_pair(KD - 2)

            def down0(n, i):
                wait_new("down0", n, i, 2)
                next_h(n, i, 2, gff[:, slot_of(n, i, 2)])
                square(n, i)
                square(n, i, 1, col_of("g_final", n, i, 2))

            ffn(0, lambda: None, down0)

            def scale_ffn1():
                b = wait_filled(act, ("sum", "ffn1"))
                act.activation(ms2[:, :], psum[:, b, 4:8], ACT.Identity)
                root("ffn1")
                act.wait_ge(root2, 1)
                act.activation(rcol[:, 0:4], rcol[:, 12:16], ACT.Sqrt, bias=eps).then_inc(root2, 1)

            def down1(n, i):
                wait_new("down1", n, i, 2)
                next_h(n, i, 2, col_of("mix_norm_2", n, i, 2))
                square(n, i)

            ffn(1, scale_ffn1, down1)

            split_high(S_PROJ2 + 1)
            root("mix2")
            for s in range(S_PROJ2 + 2, S_PROJ2 + 5):
                split_high(s)
            act.wait_ge(cols_set, 4)
            for i in range(TT):
                b = wait_filled(act, ("va", i))
                act.activation(va_hi[:, i, :], psum[:, b, :], ACT.Identity, scale=rcol[:, 4 + i:5 + i]).then_inc(v_high, 1)
            split_high(S_PROJ2 + 5)
            b = wait_filled(act, "vb")
            for i in range(TT):
                act.activation(vb_hi[:, i, :], psum[:, b, P * i:P * i + P], ACT.Identity, scale=rcol[:, 4 + i:5 + i])\
                   .then_inc(v_high, 1)
            for s in range(S_QB, S_QB + 5):
                split_high(s)

            for t in range(UN2 + 5):
                if t < UN2 and t % 4 == 0:
                    split_high(S_MIX2 + t // 4 + 1)
                u = t - 3
                if 0 <= u < UN2:
                    g, kts = u // 2, unit2(u)[5]
                    if g >= 2:
                        wait_filled(act, ("o2", g - 2))
                    b = wait_filled(act, ("t2", u))
                    act.activation(wt2_hi[:, g % 2, kts[0]:kts[-1] + 1, P * (u % 2):P * (u % 2) + P],
                                   psum[:, b, 0:P * len(kts)].rearrange("p (k q) -> p k q", q=P), ACT.Copy)\
                       .then_inc(wt2_high, 1)
                if t >= 6 and t % 2 == 0:
                    g = (t - 6) // 2
                    windowed, c, j = unit2(2 * g)[0:3]
                    r, a = DH * j, g % 2
                    y_ = yb_hi if windowed else ya_hi
                    b = wait_filled(act, ("o2", g))
                    act.activation(y_[r:r + DH, c, 2 * P * a:2 * P * a + 2 * P], psum[r:r + DH, b, 0:2 * P], ACT.Copy)\
                       .then_inc(y2_high, 1)
                if t < UN2:
                    windowed, _, _, _, head, kts = unit2(t)
                    w = P * len(kts)
                    act.wait_ge(scored2, t + 1)
                    act.activation(p2[:, t % 3, 0:w], p2[:, t % 3, 0:w], ACT.Exp, bias=stat[:, t % 3, 0:1],
                                   scale=-1.0, accum_out=stat[:, t % 3, 2:3]).then_inc(expd2, 1)
                    if windowed:
                        act.activation(stat[:, t % 3, 6:7], stat[:, t % 3, 0:1], ACT.Exp, bias=sink[:, head:head + 1])\
                           .then_inc(expd2, 1)

            def gates(n, i=None):
                act.wait_ge(sb_set, n + 1 if i is None else i + 1)
                act.activation(t_sb[:, :], t_sb[:, :], ACT.Sigmoid).then_inc(sa_set, 1)
                act.activation(t_sa[:, :], za[:, slot_of(n, i), :], ACT.Sigmoid).then_inc(sa_set, 1)
                split_high(S_MERGE + 2 * n + 2, i, 2)
                if n < KD - 1:
                    split_high(S_MERGE + 2 * n + 3, i, 2)
                act.wait_ge(merged, n + 1 if i is None else i + 1)
                act.activation(m_hi[:, slot_of(n, i), :], t_m[:, :], ACT.Identity).then_inc(m_high, 1)

            split_high(S_MERGE + 1)
            with repeat(act, KD - 1, []) as i:
                gates(0, i)
            gates(KD - 1)

            out_chunks("out2", S_OUT2, "ffn2_norm_2")

            def down2(n, i):
                wait_new("down2", n, i, 2)
                square(n, i)
                act.activation(o_scaled[:, slot_of(n, i, 2), :], x[:, slot_of(n, i, 2), :], ACT.Identity,
                               scale=col_of("final_norm_2", n, i, 2)).then_inc(o_final, 1)

            ffn(2, lambda: root("ffn2"), down2, last=True)
            root("last")
            act.wait_ge(cols_set, 6)
            for i in range(TT):
                b = wait_filled(act, ("fin", i, 0))
                act.activation(o_tok[:, i, 0:T], psum[:, b, :], ACT.Identity, scale=rcol[:, 4 + i:5 + i])\
                   .then_inc(tok_set[0], 1)

        @block.vector
        def _(dve):
            steps = Count()

            def done(ins_):
                ins_.then_inc(dve_step, 1)
                steps.n += 1
                dve.wait_ge(dve_step, steps.now())

            for at, value in ((eps, EPS), (mean_d, 1.0 / D), (one_col, 1.0), (small[0:DH, 12:13], 1.0 / DH),
                              (small[DH:P, 12:13], 0.0), (small[0:DH, 13:14], 0.0), (small[DH:P, 13:14], 1.0 / DH)):
                dve.memset(at, value).then_inc(consts_set, 1)
            b = wait_filled(dve, "vectors")
            dve.tensor_copy(vcol[:, 0:N_ROWS], psum[:, b, 0:N_ROWS]).then_inc(emptied[b], 1)
            for k in range(KD):
                b = wait_filled(dve, ("x", k))
                dve.tensor_copy(x[:, k, :], psum[:, b, :]).then_inc(emptied[b], 1)
            dve.wait_ge(cact_set, 1)
            wait_emptied(dve, "vectors")
            dve.wait_ge(x_root, 1)
            done(dve.reciprocal(rcol[:, 8:12], rcol[:, 4:8]))
            for i in range(TT):
                dve.tensor_scalar(xn_tok[:, i, :], x_tok[:, i, :], rcol[:, 8 + i:9 + i], None, ALU.mult).then_inc(xn_set, 1)
            def lambda_and_gains():
                dve.wait_ge(lam_landed, 80)
                done(dve.tensor_tensor(lamrow[:, 128:192], lamrow[:, 0:64], lamrow[:, 64:128], ALU.mult))
                dve.tensor_reduce(lamrow[:, 192:194], lamrow[:, 128:192].rearrange("p (a d) -> p a d", a=2),
                                  mybir.AxisListType.X, ALU.add).then_inc(lam_prod, 1)
                dve.tensor_scalar(neg_sink, sink, -1.0, None, ALU.mult).then_inc(lam_set, 1)
                dve.wait_ge(lam_exp, 1)
                dve.scalar_tensor_tensor(out=neg_lam, in0=lamrow[:, 195:196], scalar=-LAMBDA_INIT, in1=lamrow[:, 194:195],
                                         op0=ALU.add, op1=ALU.subtract).then_inc(lam_set, 1)
                s0 = ROW_OF["g_subln"]
                dve.tensor_scalar(sub8[:, :], vcol[:, s0:s0 + 4], 1.0 - LAMBDA_INIT, None, ALU.mult).then_inc(lam_set, 1)
                g0, f0 = ROW_OF["g_final"], ROW_OF["ffn1_norm_2"]
                dve.tensor_tensor(gff[:, :], vcol[:, g0:g0 + KD], vcol[:, f0:f0 + KD], ALU.mult).then_inc(lam_set, 1)

            for j in range(2):
                dve.wait_ge(ada_landed[2 + j], 16)
                at = first_acc[:, T * j:T * j + T]
                done(dve.tensor_scalar(at, ada_w[:, 2 + j, 0:T], cact[:, 0:1], None, ALU.mult))
                for k in range(1, KD):
                    last = dve.scalar_tensor_tensor(out=at, in0=ada_w[:, 2 + j, T * k:T * k + T], scalar=cact[:, k:k + 1],
                                                    in1=at, op0=ALU.mult, op1=ALU.add)
                    if k < KD - 1:
                        done(last)
                last.then_inc(scale_summed, 1)
                if j == 0:
                    lambda_and_gains()
            def mod_group(j, n):
                b = wait_filled(dve, ("mod", j))
                dve.tensor_tensor(modc[:, KD * j:KD * j + n], psum[:, b, 0:n], vcol[:, KD * j:KD * j + n], ALU.add)\
                   .then_inc(emptied[b], 1)
                wait_emptied(dve, ("mod", j))

            def mod_scale(dst, at, g):
                dve.scalar_tensor_tensor(out=dst[:, :], in0=modc[:, at:at + KD], scalar=1.0,
                                         in1=vcol[:, ROW_OF[g]:ROW_OF[g] + KD], op0=ALU.add, op1=ALU.mult).then_inc(mod_set, 1)

            mod_group(0, 2 * KD)
            mod_scale(scale1, SC1, "g_mix")

            def split_low(s, i=None, step=1):
                dve.wait_ge(w_high, s + 1 if i is None else i * step + s + 1)
                n = tiles_of(s) * P
                dve.tensor_tensor(w_lo[:, s % 2, 0:n], w_raw[:, s % 2, 0:n], w_hi[:, s % 2, 0:n].bitcast(F32),
                                  ALU.subtract).then_inc(w_ready, 1)

            def low(dst, whole_, high, n, i=None, step=1):
                dve.wait_ge(h_high, n + 1 if i is None else i * step + n + 1)
                dve.tensor_tensor(dst, whole_, high.bitcast(F32), ALU.subtract).then_inc(h_ready, 1)

            dve.wait_ge(mod_set, 1)
            for k in range(KD):
                m = k % 2
                wait_emptied(dve, ("xn", k))
                done(dve.tensor_scalar(hm[:, m, :], xn_t[:, k, :], scale1[:, k:k + 1], modc[:, SH1 + k:SH1 + k + 1],
                                       ALU.mult, ALU.add))
                low(h_lo[:, k, :], hm[:, m, :], h_hi[:, k, :], k)
                if k in (0, 2):
                    split_low(k // 2)
            for s in range(2, 5):
                split_low(s)
            for i in range(TT):
                b = bank[("v1", i)]
                dve.wait_ge(v_high, i + 1)
                dve.tensor_tensor(v1_lo[:, i, :], psum[:, b, :], v1_hi[:, i, :].bitcast(F32), ALU.subtract)\
                   .then_inc(emptied[b], 1)
            split_low(5)
            mod_group(GT1 // KD, KD)
            split_low(6)

            for t in range(UN1 + 5):
                if t - 1 in MOD_STEP:
                    mod_group(MOD_STEP[t - 1], KD)
                if t - 1 in MOD_STEP and MOD_STEP[t - 1] == SC2 // KD:
                    mod_scale(scale2, SC2, "g_ffn")
                if t < 2 * N_MIX1 and t % 2 == 0:
                    split_low(S_MIX1 + t // 2 + 1)
                if 2 <= t <= 2 * N_MIX1 and t % 2 == 0:
                    j = t // 2 - 1
                    kind, c = KINDS1[j]
                    if kind == "xc":
                        wait_emptied(dve, ("slab", S_MIX1 + KINDS1.index(("cg", c))))
                        dve.wait_ge(pads_set, 1)
                        b = wait_filled(dve, ("slab", S_MIX1 + j))
                        dve.tensor_tensor(conv_u[:, c, 1:T + 1], psum[:, b, :], conv_c[:, c, :], ALU.mult)\
                           .then_inc(emptied[b], 1)
                    elif kind == "bg":
                        dve.wait_ge(conved, c + 1)
                        b = wait_filled(dve, ("slab", S_MIX1 + j))
                        dve.tensor_tensor(y_side[:, 2 + c, :], psum[:, b, :], conv_c[:, c, :], ALU.mult)\
                           .then_inc(emptied[b], 1)
                if t < UN1:
                    h, i = t // 4, t % 4
                    if i == 0:
                        dve.wait_ge(alibi_set, h + 1)
                    if t >= 3:
                        wait_filled(dve, ("t1", t - 3))
                    for m in range(2):
                        b = wait_filled(dve, ("s1", t, m))
                        dve.tensor_tensor_reduce(p1[:, t % 3, m, :], psum[:, b, :],
                                                 alibi[:, h % 2, T - P - P * i:2 * T - P - P * i], 1.0, 3e38,
                                                 ALU.add, ALU.min, stat[:, t % 3, m:m + 1]).then_inc(emptied[b], 1)
                u = t - 1
                if 0 <= u < UN1:
                    st, n = stat[:, u % 3, :], u % 3
                    dve.wait_ge(expd, 2 * u + 2)
                    if u == 0:
                        dve.wait_ge(lam_set, 4)
                    done(dve.reciprocal(st[:, 4:6], st[:, 2:4]))
                    done(dve.tensor_scalar(p1[:, n, 1, :], p1[:, n, 1, :], st[:, 5:6], neg_lam, ALU.mult, ALU.mult))
                    dve.scalar_tensor_tensor(out=p1[:, n, 0, :], in0=p1[:, n, 0, :], scalar=st[:, 4:5],
                                             in1=p1[:, n, 1, :], op0=ALU.mult, op1=ALU.add).then_inc(combined, 1)
                u = t - 3
                if 0 <= u < UN1:
                    b = bank[("t1", u)]
                    at = slice(P * (u % 2), P * (u % 2) + P)
                    dve.wait_ge(wt_high, u + 1)
                    dve.tensor_tensor(wt_lo[:, u // 2 % 2, :, at], psum[:, b, :].rearrange("p (k q) -> p k q", k=TT),
                                      wt_hi[:, u // 2 % 2, :, at].bitcast(F32), ALU.subtract).then_inc(emptied[b], 1)
                if t in (UN1, UN1 + 4):
                    for n, c in enumerate((2, 3) if t == UN1 else (0, 1)):
                        low(h_lo[:, 4 + c, :], y_side[:, c, :], h_hi[:, 4 + c, :], (8 if t == UN1 else 10) + n)
            split_low(S_OUT1 + 1)
            wait_emptied(dve, "sub_sum")
            dve.reciprocal(rsub[:, :], rsub[:, :]).then_inc(sub_scaled, 1)
            wait_emptied(dve, ("o1", UN1 // 2 - 1))
            for c in range(5):
                if c < 4:
                    b = wait_filled(dve, ("sub", c))
                    dve.scalar_tensor_tensor(out=k1[:, c, :], in0=o1[:, c, :], scalar=sub8[:, c:c + 1],
                                             in1=psum[:, b, :], op0=ALU.mult, op1=ALU.mult).then_inc(y_set, 1)
                if c:
                    dve.wait_ge(y_set, c)
                    low(h_lo[:, c - 1, :], k1[:, c - 1, :], h_hi[:, c - 1, :], 11 + c)

            def col_of(name, n, i, step):
                return vcol[:, slot_of(ROW_OF[name] + n, i, step)]

            def wait_new(phase, n, i, step):
                v = NEW_X[phase] + n + 1
                dve.wait_ge(x_new, v if i is None else i * step + v)

            def add_gated(name, phase, n, i, gt):
                b = wait_filled(dve, name, n, i, 2)
                at = slot_of(n, i, 2)
                dve.scalar_tensor_tensor(out=x[:, at, :], in0=psum[:, b:b + 1, :], scalar=modc[:, slot_of(gt + n, i, 2)],
                                         in1=x[:, at, :], op0=ALU.mult, op1=ALU.add).then_inc(x_new, 1)
                wait_new(phase, n, i, 2)

            def next_low(phase, gen, n, i, col):
                at = slot_of(n, i, 2)
                v = 8 * gen + n + 1
                dve.wait_ge(h_high, v if i is None else i * 2 + v)
                dve.scalar_tensor_tensor(out=h_lo[:, at, :], in0=x[:, at, :], scalar=col, in1=h_hi[:, at, :].bitcast(F32),
                                         op0=ALU.mult, op1=ALU.subtract).then_inc(h_ready, 1)

            def out1_pair(n0, i=None):
                for n in (n0, n0 + 1):
                    if n:
                        split_low(S_OUT1 + n + 1, i, 2)
                    add_gated(("out1",), "out1", n, i, GT1)

            out1_pair(0)
            with repeat(dve, KD // 2 - 1, []) as i:
                out1_pair(2, i)

            def token_scale(name):
                wait_emptied(dve, ("sum", name))
                dve.reciprocal(rcol[:, 4:8], rcol[:, 0:4]).then_inc(cols_set, 1)

            def take_scale(name):
                b = wait_filled(dve, ("scale", name))
                dve.tensor_copy(rs[:, :], psum[:, b, :]).then_inc(scale_set, 1)
                dve.wait_ge(*free_at[("scale", name)])
                done(dve.tensor_scalar(rs_half[:, :], rs[:, :], 0.5, None, ALU.mult))

            token_scale("ffn0")
            b = wait_filled(dve, ("scale", "ffn0"))
            dve.wait_ge(mod_set, 2)
            for k in range(KD + 1):
                if k < KD:
                    if k >= 2:
                        dve.wait_ge(h_high, 8 * GEN["ffn0"] + k - 1)
                    dve.tensor_tensor(x_scaled[:, k % 2, :], x[:, k, :], psum[:, b, :], ALU.mult).then_inc(scaled_x, 1)
                if k:
                    j = k - 1
                    dve.wait_ge(h_whole, j + 1)
                    low(h_lo[:, j, :], h_full[:, j % 2, :], h_hi[:, j, :], 8 * GEN["ffn0"] + j)

            def ffn(f, between, before_down, down, last=False):
                s0 = S_GU[f]

                def pair(n, i=None):
                    split_low(s0 + 2 * n + 1, i, 2)
                    if n == 0:
                        between()
                    if f:
                        b = wait_filled(dve, ("gate", f), n, i)
                        dve.tensor_tensor(t_gate[:, :], psum[:, b, :], rs[:, :], ALU.mult).then_inc(gate_scaled, 1)
                    split_low(s0 + 2 * n + 2, i, 2)
                    v = KF * f + n + 1
                    dve.wait_ge(gate_act, v if i is None else i + v)
                    b = wait_filled(dve, ("up", f), n, i)
                    dve.tensor_tensor(t_hid[:, :], psum[:, b, :], t_silu[:, :], ALU.mult).then_inc(hid_set, 1)
                    dve.wait_ge(hid_set, v if i is None else i + v)
                    dve.wait_ge(hid_high, v if i is None else i + v)
                    at = slot_of(n, i)
                    dve.tensor_tensor(hid_lo[:, at, :], t_hid[:, :], hid_hi[:, at, :].bitcast(F32), ALU.subtract)\
                       .then_inc(hid_ready, 1)

                pair(0)
                with repeat(dve, KF - 2, []) as i:
                    pair(1, i)
                pair(KF - 1)
                before_down()

                def down_pair(n0, i=None):
                    for n in (n0, n0 + 1):
                        s = S_DN[f] + 2 * n
                        split_low(s + 1, i, 4)
                        if not (last and n == KD - 1):
                            split_low(s + 2, i, 4)
                        down(n, i)

                with repeat(dve, KD // 2 - 1, [(steps, 2 if f == 1 else 0)]) as i:
                    down_pair(0, i)
                down_pair(KD - 2)

            def down0(n, i):
                add_gated(("down", 0), "down0", n, i, GT2)
                next_low("down0", GEN["ffn1"], n, i, gff[:, slot_of(n, i, 2)])

            ffn(0, lambda: None, lambda: mod_group(GT2 // KD, KD), down0)

            def scale_ffn1():
                wait_emptied(dve, ("sum", "ffn1"))
                dve.reciprocal(rcol[:, 8:12], rcol[:, 0:4]).then_inc(cols_set, 1)
                dve.wait_ge(cols_set, 2)
                done(dve.tensor_tensor(rcol[:, 12:16], ms2[:, :], rcol[:, 8:12], ALU.mult))
                dve.tensor_tensor(rcol[:, 12:16], rcol[:, 12:16], rcol[:, 8:12], ALU.mult).then_inc(root2, 1)
                dve.wait_ge(root2, 2)
                done(dve.reciprocal(rcol[:, 4:8], rcol[:, 0:4]))
                dve.tensor_tensor(rcol[:, 4:8], rcol[:, 4:8], rcol[:, 8:12], ALU.mult).then_inc(cols_set, 1)
                b = wait_filled(dve, ("scale", "ffn1"))
                dve.tensor_copy(rs_fin[:, :], psum[:, b, :]).then_inc(emptied[b], 1)
                b = wait_filled(dve, ("scale2", "ffn1"))
                dve.tensor_copy(rs[:, :], psum[:, b, :]).then_inc(scale_set, 1)
                dve.wait_ge(*free_at[("scale2", "ffn1")])
                done(dve.tensor_scalar(rs_half[:, :], rs[:, :], 0.5, None, ALU.mult))

            def add_scaled(name, phase, n, i):
                b = wait_filled(dve, name, n, i, 2)
                at = slot_of(n, i, 2)
                dve.tensor_tensor(t_gate[:, :], psum[:, b, :], rs_half[:, :], ALU.mult).then_inc(t_set, 1)
                v = {"down1": 0, "down2": KD}[phase] + n + 1
                dve.wait_ge(t_set, v if i is None else i * 2 + v)
                dve.tensor_tensor(x[:, at, :], t_gate[:, :], x[:, at, :], ALU.add).then_inc(x_new, 1)
                wait_new(phase, n, i, 2)

            def down1(n, i):
                at = slot_of(n, i, 2)
                done(dve.scalar_tensor_tensor(out=x[:, at, :], in0=x[:, at, :], scalar=col_of("g_final", n, i, 2),
                                              in1=rs_fin[:, :], op0=ALU.mult, op1=ALU.mult))
                add_scaled(("down", 1), "down1", n, i)
                next_low("down1", GEN["mix2"], n, i, col_of("mix_norm_2", n, i, 2))

            ffn(1, scale_ffn1, lambda: None, down1)

            split_low(S_PROJ2 + 1)
            token_scale("mix2")
            take_scale("mix2")
            for s in range(S_PROJ2 + 2, S_PROJ2 + 5):
                split_low(s)
            for i in range(TT):
                b = bank[("va", i)]
                dve.wait_ge(v_high, TT + i + 1)
                dve.scalar_tensor_tensor(out=va_lo[:, i, :], in0=psum[:, b, :], scalar=rcol[:, 4 + i:5 + i],
                                         in1=va_hi[:, i, :].bitcast(F32), op0=ALU.mult, op1=ALU.subtract)\
                   .then_inc(emptied[b], 1)
            split_low(S_PROJ2 + 5)
            b = bank["vb"]
            dve.wait_ge(v_high, 3 * TT)
            for i in range(TT):
                last = dve.scalar_tensor_tensor(out=vb_lo[:, i, :], in0=psum[:, b, P * i:P * i + P],
                                                scalar=rcol[:, 4 + i:5 + i], in1=vb_hi[:, i, :].bitcast(F32),
                                                op0=ALU.mult, op1=ALU.subtract)
            last.then_inc(emptied[b], 1)

            def embed(name, dst):
                b = wait_filled(dve, name)
                dve.tensor_tensor(z_t, psum[:, b, :], sin_sb[:, :], ALU.mult).then_inc(emptied[b], 1)
                done(dve.tensor_tensor(z_c, dst, cos_sb[:, :], ALU.mult))
                wait_emptied(dve, name)
                dve.tensor_tensor(dst, z_t, z_c, ALU.add).then_inc(roped, 1)

            split_low(S_QB)
            dve.wait_ge(table_landed, 64)
            b = wait_filled(dve, "kb")
            dve.tensor_tensor(kb[:, :], psum[:, b, :], rs[:, :], ALU.mult).then_inc(roped, 1)
            dve.wait_ge(roped, 1)
            for c in range(4):
                split_low(S_QB + c + 1)
                if c == 0:
                    embed("kb_turn", kb[:, :])
                else:
                    embed(("qb_turn", c - 1), qb[:, c - 1, :])
                b = wait_filled(dve, ("qb", c))
                dve.scalar_tensor_tensor(out=qb[:, c, :], in0=psum[:, b, :], scalar=-float(DH) ** -0.5, in1=rs[:, :],
                                         op0=ALU.mult, op1=ALU.mult).then_inc(roped, 1)
                dve.wait_ge(roped, 3 + 2 * c)
            embed(("qb_turn", 3), qb[:, 3, :])

            for t in range(UN2 + 5):
                if t < UN2:
                    windowed, c, j, i, head, kts = unit2(t)
                    w, st = P * len(kts), stat[:, t % 3, :]
                    if t >= 3:
                        wait_filled(dve, ("t2", t - 3))
                    b = wait_filled(dve, ("s2", t))
                    if windowed:
                        off = P * (kts[0] - (i - 1))
                        bias = band[:, off:off + w]
                    else:
                        if i == 0:
                            dve.wait_ge(near_set, head + 1)
                        at = DR // 2 - 1 - 2 * i
                        bias = near[:, head % 2, at:at + NEAR_ROWS, :].rearrange("p a b -> p (a b)")
                    dve.tensor_tensor_reduce(p2[:, t % 3, 0:w], psum[:, b, 0:w], bias, 1.0, 3e38, ALU.add, ALU.min,
                                             st[:, 0:1]).then_inc(free_at[("s2", t)][0], 1)
                    if windowed:
                        wait_emptied(dve, ("s2", t))
                        dve.tensor_scalar(st[:, 0:1], st[:, 0:1], neg_sink[:, head:head + 1], None, ALU.min)\
                           .then_inc(scored2, 1)
                u = t - 1
                if 0 <= u < UN2:
                    windowed, w, st = unit2(u)[0], P * len(unit2(u)[5]), stat[:, u % 3, :]
                    dve.wait_ge(expd2, exps2(u))
                    if windowed:
                        done(dve.tensor_tensor(st[:, 2:3], st[:, 2:3], st[:, 6:7], ALU.add))
                    done(dve.reciprocal(st[:, 4:5], st[:, 2:3]))
                    dve.tensor_scalar(p2[:, u % 3, 0:w], p2[:, u % 3, 0:w], st[:, 4:5], None, ALU.mult)\
                       .then_inc(combined2, 1)
                if 6 <= t <= UN2 + 2 and t % 4 == 2:
                    j = t // 4 - 1
                    b = wait_filled(dve, ("slab", S_MIX2 + j))
                    if j < 8 and j % 2 == 0:
                        dve.scalar_tensor_tensor(out=qa[:, j // 2, :], in0=psum[:, b, :], scalar=-float(DH) ** -0.5,
                                                 in1=rs[:, :], op0=ALU.mult, op1=ALU.mult).then_inc(emptied[b], 1)
                    else:
                        dst = ka[:, j // 2, :] if j < 8 else za[:, j - 8, :]
                        dve.tensor_tensor(dst, psum[:, b, :], rs[:, :], ALU.mult).then_inc(emptied[b], 1)
                u = t - 3
                if 0 <= u < UN2:
                    kts = unit2(u)[5]
                    b = bank[("t2", u)]
                    at = (slice(None), u // 2 % 2, slice(kts[0], kts[-1] + 1), slice(P * (u % 2), P * (u % 2) + P))
                    dve.wait_ge(wt2_high, u + 1)
                    dve.tensor_tensor(wt2_lo[at], psum[:, b, 0:P * len(kts)].rearrange("p (k q) -> p k q", q=P),
                                      wt2_hi[at].bitcast(F32), ALU.subtract).then_inc(emptied[b], 1)
                if t >= 6 and t % 2 == 0:
                    g = (t - 6) // 2
                    windowed, c, j = unit2(2 * g)[0:3]
                    r, a = DH * j, g % 2
                    y_, yl = (yb_hi, yb_lo) if windowed else (ya_hi, ya_lo)
                    at = (slice(r, r + DH), c, slice(2 * P * a, 2 * P * a + 2 * P))
                    b = bank[("o2", g)]
                    dve.wait_ge(y2_high, g + 1)
                    dve.tensor_tensor(yl[at], psum[r:r + DH, b, 0:2 * P], y_[at].bitcast(F32), ALU.subtract)\
                       .then_inc(emptied[b], 1)
                if t < UN2 and t % 4 == 1:
                    split_low(S_MIX2 + t // 4 + 1)

            def merge(n, i=None):
                def at(slope, v):
                    return v if i is None else i * slope + v

                b = wait_filled(dve, ("gb",), n, i)
                dve.tensor_tensor(t_sb[:, :], psum[:, b, :], rs[:, :], ALU.mult).then_inc(sb_set, 1)
                split_low(S_MERGE + 2 * n + 2, i, 2)
                dve.wait_ge(sa_set, at(2, 2 * n + 2))
                for key, t_ in (("a", t_sa), ("b", t_sb)):
                    b = wait_filled(dve, (key,), n, i)
                    dve.tensor_tensor(t_[:, :], psum[:, b, :], t_[:, :], ALU.mult).then_inc(branch_set, 1)
                dve.wait_ge(branch_set, at(2, 2 * n + 2))
                dve.tensor_tensor(t_m[:, :], t_sa[:, :], t_sb[:, :], ALU.add).then_inc(merged, 1)
                if n < KD - 1:
                    split_low(S_MERGE + 2 * n + 3, i, 2)
                dve.wait_ge(merged, at(1, n + 1))
                dve.wait_ge(m_high, at(1, n + 1))
                dve.tensor_tensor(m_lo[:, slot_of(n, i), :], t_m[:, :], m_hi[:, slot_of(n, i), :].bitcast(F32),
                                  ALU.subtract).then_inc(m_ready, 1)

            split_low(S_MERGE + 1)
            with repeat(dve, KD - 1, []) as i:
                merge(0, i)
            merge(KD - 1)

            with repeat(dve, KD // 2, []) as i:
                for n in range(2):
                    split_low(S_OUT2 + n + 1, i, 2)
                    b = wait_filled(dve, ("out2",), n, i, 2)
                    at = slot_of(n, i, 2)
                    dve.tensor_tensor(x[:, at, :], psum[:, b:b + 1, :], x[:, at, :], ALU.add).then_inc(x_new, 1)
                    wait_new("out2", n, i, 2)
                    next_low("out2", GEN["ffn2"], n, i, col_of("ffn2_norm_2", n, i, 2))

            def scale_ffn2():
                token_scale("ffn2")
                take_scale("ffn2")

            ffn(2, scale_ffn2, lambda: None, lambda n, i: add_scaled(("down", 2), "down2", n, i), last=True)
            token_scale("last")
            dve.wait_ge(cols_set, 6)
            for i in range(TT):
                b = wait_filled(dve, ("fin", i, 1))
                dve.tensor_scalar(o_tok[:, i, T:D], psum[:, b, :], rcol[:, 4 + i:5 + i], None, ALU.mult)\
                   .then_inc(tok_set[1], 1)

        @block.gpsimd
        def _(pool):
            steps = Count()

            def done(ins_):
                ins_.then_inc(pool_step, 1)
                steps.n += 1
                pool.wait_ge(pool_step, steps.now())

            rows_loaded = [0, 0]

            def mod_row(j, k):
                pool.dma_start(ada_row[:, k % 2, :], ins["w_ada"][0, P * k:P * k + P, D * j:D * j + D])\
                    .then_inc(row_landed[k % 2], 16)

            def mod_products(j, loaded=1):
                for k in range(KD):
                    if loaded <= k + 1 < KD:
                        mod_row(j, k + 1)
                    rows_loaded[k % 2] += 16
                    pool.wait_ge(row_landed[k % 2], rows_loaded[k % 2])
                    if k == 0:
                        done(pool.tensor_tensor(mod_acc, ada_row[:, 0, :], cact[:, 0:1].to_broadcast([P, D]), ALU.mult))
                    else:
                        done(pool.tensor_tensor(ada_row[:, k % 2, :], ada_row[:, k % 2, :],
                                                cact[:, k:k + 1].to_broadcast([P, D]), ALU.mult))
                        last = pool.tensor_tensor(mod_acc, mod_acc, ada_row[:, k % 2, :], ALU.add)
                        if k + 1 < KD:
                            done(last)
                last.then_inc(mod_summed, 1)
                pool.wait_ge(mod_summed, j - 1)

            for k in range(2):
                mod_row(GT1 // KD, k)
            pool.wait_ge(cact_set, 1)
            mod_products(GT1 // KD, 2)
            pool.dma_start(rpb_rows, ins["rpb"].unsqueeze(0).to_broadcast([GRID, n_rpb])).then_inc(rpb_copied, 16)
            pool.wait_ge(h_ready, KD)
            done(pool.memset(wpool_bd[:, :, :], 0.0))
            for g in range(4):
                r = DH * (g % 2)
                pool.dma_start(wpool_bd[r:r + DH, g // 2, r:r + DH], ins["w_pool"][0, g]).then_inc(wpool_landed, 16)
            done(pool.memset(pool_u[:, :], 0.0))
            done(pool.memset(conv_u[:, :, :], 0.0))
            pool.memset(pool_s[:, :, 0:1], 0.0).then_inc(pads_set, 1)
            mod_row(SH2 // KD, 0)
            wait_filled(pool, ("mod", GT1 // KD))
            mod_products(SH2 // KD)
            pool.wait_ge(count_landed, 32)

            def window_sum(dst, src, reach, lo, hi):
                left, right = (1, 0) if reach == 0 else (reach, reach)
                done(pool.tensor_tensor(dst[:, lo:hi], src[:, lo - left:hi - left], src[:, lo + right:hi + right], ALU.add))

            for c, dst in enumerate((pool_d, pool_t)):
                wait_emptied(pool, ("slab", S_MIX1 + KINDS1.index(("u", c))))
                sa_, sb_ = pool_s[:, 0, :], pool_s[:, 1, :]
                window_sum(sa_, pool_u, 0, 1, T + 15)
                window_sum(sb_, sa_, 1, 2, T + 14)
                if c == 1:
                    window_sum(sa_, sb_, 2, 4, T + 12)
                    window_sum(sb_, sa_, 4, 8, T + 8)
                for half in range(2):
                    r = slice(DH * half, DH * half + DH)
                    done(pool.tensor_tensor(dst[r, :], pool_s[r, half, 8:8 + T], count_sb[c][r, :], ALU.mult))
                pool.tensor_tensor(dst[:, :], dst[:, :], pool_u[:, 8:8 + T], ALU.subtract).then_inc(pooled, 1)
                pool.wait_ge(pooled, c + 1)
            mod_row(SC2 // KD, 0)
            wait_filled(pool, ("mod", SH2 // KD))
            mod_products(SC2 // KD)
            w0 = ROW_OF["conv_w"]
            for c in range(2):
                wait_emptied(pool, ("slab", S_MIX1 + KINDS1.index(("xc", c))))
                taps = [vcol[:, w0 + 2 * j + c:w0 + 2 * j + c + 1].to_broadcast([P, T]) for j in range(3)]
                done(pool.tensor_tensor(conv_c[:, c, :], conv_u[:, c, 0:T], taps[0], ALU.mult))
                for j in (1, 2):
                    done(pool.tensor_tensor(pool_s[:, 0, 0:T], conv_u[:, c, j:T + j], taps[j], ALU.mult))
                    last = pool.tensor_tensor(conv_c[:, c, :], conv_c[:, c, :], pool_s[:, 0, 0:T], ALU.add)
                    if j == 1:
                        done(last)
                last.then_inc(conved, 1)
                pool.wait_ge(conved, c + 1)

            def sums(phase, clear, kinds=1):
                if clear:
                    wait_filled(pool, ("sum", clear))
                    done(pool.memset(acc[:, 0:kinds, :], 0.0))
                else:
                    pool.memset(acc[:, 0:kinds, :], 0.0).then_inc(summed, SUM0)
                    pool.wait_ge(summed, SUM0)
                with repeat(pool, KD // 2, []) as i:
                    for n in range(2):
                        for m in range(kinds):
                            v = SQUARES[phase] + kinds * n + m + 1
                            pool.wait_ge(squared, i * 2 * kinds + v)
                            pool.tensor_tensor(acc[:, m, :], acc[:, m, :], sq[:, n, m, :], ALU.add).then_inc(summed, 1)
                            pool.wait_ge(summed, i * 2 * kinds + v + SUM0)

            wait_filled(pool, ("mod", SC2 // KD))
            sums("out1", None)
            mod_row(GT2 // KD, 0)
            wait_filled(pool, ("sum", "ffn0"))
            mod_products(GT2 // KD)
            wait_filled(pool, ("mod", GT2 // KD))
            sums("down0", "ffn0", 2)
            pool.wait_ge(hid_ready, 2 * KF)
            for dst, name in ((sin_sb, "k_sin"), (band, "k_band"), (near_mask, "k_near")):
                pool.dma_start(dst[:, :], ins[name]).then_inc(table_landed, 16)
            sums("down1", "ffn1")
            pool.wait_ge(x_new, NEW_X["down1"] + KD)
            pool.dma_start(cos_sb[:, :], ins["k_cos"]).then_inc(table_landed, 16)

            def near_load(h):
                for odd in range(2):
                    at = PAD + h * DR * DC + (1 - odd) * DC + NEAR_COLS - 1
                    src = bass.AP(tensor=rpb_rows.tensor, offset=at, ap=[[n_rpb - 1, GRID], [DC, DR - 1], [1, GRID]])
                    pool.dma_start(near[GRID * odd:GRID * odd + GRID, h % 2, :, :], src).then_inc(near_landed[h % 2], 16)

            pool.wait_ge(table_landed, 64)
            pool.wait_ge(rpb_copied, 16)
            near_load(0)
            near_load(1)
            for h in range(H):
                if h >= 2:
                    wait_emptied(pool, ("s2", UN2 // 2 + 4 * (h - 2) + 3))
                    near_load(h)
                pool.wait_ge(near_landed[h % 2], 32 * (h // 2 + 1))
                pool.tensor_tensor(near[:, h % 2, :, :], near_mask[:, :].unsqueeze(1).to_broadcast([P, DR - 1, GRID]),
                                   near[:, h % 2, :, :], ALU.subtract).then_inc(near_set, 1)
            sums("out2", "mix2")
            sums("down2", "ffn2")


def kernel(**inputs):
    from concourse import bacc
    from concourse.bass_utils import run_bass_kernel_spmd

    vectors = {name for name, _ in VECTORS}
    arrays = {}
    for name, a in inputs.items():
        a = np.asarray(a)
        if name == "c" or name in vectors:
            a = a.reshape(-1, P)
        elif name == "na_rpb_2":
            name, a = "rpb", np.concatenate([np.zeros(PAD, a.dtype), a.reshape(-1), np.zeros(GRID + DC, a.dtype)])
        arrays[name] = np.ascontiguousarray(a)
    arrays.update(constants())
    nc = bacc.Bacc("TRN2", target_bir_lowering=False, num_devices=1)
    named = {f"in_{k}": v for k, v in arrays.items()}
    ins = {k[3:]: nc.dram_tensor(k, v.shape, mybir.dt.from_np(v.dtype), kind="ExternalInput").ap()
           for k, v in named.items()}
    out = nc.dram_tensor("out_0", (1, T, D), F32, kind="ExternalOutput").ap()
    program(nc, ins, out)
    r = run_bass_kernel_spmd(nc, [named], core_ids=[0])
    return r.results[0]["out_0"]
```
